# Optimizing a Trainium2 kernel written in Bass

```python
import math
import jax, jax.numpy as jnp
from jax import lax
import numpy as np

D_MODEL = 2048
BATCH = 1
SEQ = 256
DEPTH = 1

D_FF = 5504
SSD_D_INNER = 2048
SSD_HEAD_DIM = 64
SSD_HEADS = SSD_D_INNER // SSD_HEAD_DIM
SSD_GROUPS = 4
SSD_HEADS_PER_GROUP = SSD_HEADS // SSD_GROUPS
SSD_STATE = 128
SSD_CONV = 4
SSD_CHUNK = 128
SSD_CONV_DIM = SSD_D_INNER + 2 * SSD_GROUPS * SSD_STATE
S5_WIDTH = 1024
S5_GROUP_SIZE = 16
S5_GROUPS = S5_WIDTH // S5_GROUP_SIZE
S5_STATE = 64
OFF_XBC = SSD_D_INNER
OFF_DT = OFF_XBC + SSD_CONV_DIM
OFF_U = OFF_DT + SSD_HEADS
OFF_GATES = OFF_U + S5_WIDTH
IN_COLS = OFF_GATES + 2 * D_MODEL
N_ADA = 9
EPS = 1e-6

kernel_name = "hybrid_ssd_s5_gated_macaron_block"

def rms_norm(x, g):
    xf = x.astype(jnp.float32)
    y = xf * lax.rsqrt(jnp.mean(xf * xf, axis=-1, keepdims=True) + EPS)
    return (y * g.astype(jnp.float32)).astype(x.dtype)

def modulate(x, g, shift, scale):
    return rms_norm(x, g) * (1 + scale) + shift

def swiglu(h, w_in, w_out):
    a, b = jnp.split(h @ w_in, 2, axis=-1)
    return (jax.nn.silu(a) * b) @ w_out

def causal_depthwise_conv(x, w, b):
    k_w = w.shape[0]
    s = x.shape[1]
    xp = jnp.pad(x, ((0, 0), (k_w - 1, 0), (0, 0)))
    out = b
    for k in range(k_w):
        out = out + xp[:, k:k + s] * w[k]
    return out

def ssd_mixer(xbc, z, dt_raw, conv_w, conv_b, dt_bias, a_log, d_skip, norm_w):
    f32 = jnp.float32
    bsz, s, _ = xbc.shape
    nc = s // SSD_CHUNK
    G, R, P, N, L = SSD_GROUPS, SSD_HEADS_PER_GROUP, SSD_HEAD_DIM, SSD_STATE, SSD_CHUNK
    xbc = jax.nn.silu(causal_depthwise_conv(xbc, conv_w, conv_b)).astype(f32)
    xs, bm, cm = jnp.split(xbc, [SSD_D_INNER, SSD_D_INNER + G * N], axis=-1)
    xs = xs.reshape(bsz, nc, L, G, R, P)
    bm = bm.reshape(bsz, nc, L, G, N)
    cm = cm.reshape(bsz, nc, L, G, N)
    dt = jax.nn.softplus(dt_raw.astype(f32) + dt_bias.astype(f32)).reshape(bsz, nc, L, G, R)
    a = -jnp.exp(a_log.astype(f32)).reshape(G, R)
    xdt = xs * dt[..., None]
    da_cs = jnp.cumsum(jnp.moveaxis(dt * a, 2, -1), axis=-1)
    causal = jnp.tril(jnp.ones((L, L), dtype=bool))
    seg = da_cs[..., :, None] - da_cs[..., None, :]
    decay_ls = jnp.exp(jnp.where(causal, seg, -jnp.inf))
    cb = jnp.einsum('bclgn,bcsgn->bcgls', cm, bm)
    y_diag = jnp.einsum('bcgls,bcgrls,bcsgrp->bclgrp', cb, decay_ls, xdt)
    decay_to_end = jnp.exp(da_cs[..., -1:] - da_cs)
    states = jnp.einsum('bclgn,bcgrl,bclgrp->bcgrpn', bm, decay_to_end, xdt)
    chunk_decay = jnp.exp(da_cs[..., -1])

    def step(h, inp):
        st, dec = inp
        return dec[..., None, None] * h + st, h

    h0 = jnp.zeros((bsz, G, R, P, N), f32)
    _, prev = lax.scan(step, h0, (jnp.moveaxis(states, 1, 0), jnp.moveaxis(chunk_decay, 1, 0)))
    prev = jnp.moveaxis(prev, 0, 1)
    y_off = jnp.einsum('bclgn,bcgrpn,bcgrl->bclgrp', cm, prev, jnp.exp(da_cs))
    y = y_diag + y_off + d_skip.astype(f32).reshape(G, R)[:, :, None] * xs
    y = y.reshape(bsz, s, G, R * P)
    yz = y * jax.nn.silu(z.astype(f32)).reshape(bsz, s, G, R * P)
    yz = yz * lax.rsqrt(jnp.mean(yz * yz, axis=-1, keepdims=True) + EPS)
    return (yz.reshape(bsz, s, SSD_D_INNER) * norm_w.astype(f32)).astype(z.dtype)

def s5_mixer(u, lambda_re, lambda_im, b_re, b_im, c_re, c_im, d_skip, log_dt):
    f32 = jnp.float32
    bsz, s, _ = u.shape
    uf = u.astype(f32).reshape(bsz, s, S5_GROUPS, S5_GROUP_SIZE)
    dt = jnp.exp(log_dt.astype(f32))[:, None]
    lr = jnp.minimum(lambda_re.astype(f32), -1e-4)
    li = lambda_im.astype(f32)
    mag = jnp.exp(lr * dt)
    ar = mag * jnp.cos(li * dt)
    ai = mag * jnp.sin(li * dt)
    den = lr * lr + li * li
    nr = ar - 1.0
    kr = (nr * lr + ai * li) / den
    ki = (ai * lr - nr * li) / den
    br = b_re.astype(f32)
    bi = b_im.astype(f32)
    bbar_re = kr[..., None] * br - ki[..., None] * bi
    bbar_im = kr[..., None] * bi + ki[..., None] * br
    bu_re = jnp.einsum('bsgi,gpi->bsgp', uf, bbar_re)
    bu_im = jnp.einsum('bsgi,gpi->bsgp', uf, bbar_im)
    a_re = jnp.broadcast_to(ar, bu_re.shape)
    a_im = jnp.broadcast_to(ai, bu_im.shape)

    def combine(e1, e2):
        a1r, a1i, b1r, b1i = e1
        a2r, a2i, b2r, b2i = e2
        return (a2r * a1r - a2i * a1i,
                a2r * a1i + a2i * a1r,
                a2r * b1r - a2i * b1i + b2r,
                a2r * b1i + a2i * b1r + b2i)

    _, _, s_re, s_im = lax.associative_scan(combine, (a_re, a_im, bu_re, bu_im), axis=1)
    y = (jnp.einsum('bsgp,gip->bsgi', s_re, c_re.astype(f32))
         - jnp.einsum('bsgp,gip->bsgi', s_im, c_im.astype(f32))
         + d_skip.astype(f32) * uf)
    return y.reshape(bsz, s, S5_WIDTH).astype(u.dtype)

def setup_inputs(seed: int = 0) -> dict:
    key = jax.random.key(seed)
    ks = jax.random.split(key, 40)
    f32 = jnp.float32

    def nrm(k, shape, scale):
        return jax.random.normal(k, shape, f32) * scale

    dt_ssd = jnp.exp(jax.random.uniform(ks[11], (DEPTH, SSD_HEADS), f32, math.log(1e-3), math.log(1e-1)))
    lam_im = (jnp.pi * jnp.arange(S5_STATE, dtype=f32))[None, None, :] + nrm(ks[16], (DEPTH, S5_GROUPS, S5_STATE), 0.01)
    return {
        "x": nrm(ks[0], (BATCH, SEQ, D_MODEL), 1.0),
        "c": nrm(ks[1], (BATCH, D_MODEL), 1.0),
        "w_ada": nrm(ks[2], (DEPTH, D_MODEL, N_ADA * D_MODEL), D_MODEL ** -0.5),
        "b_ada": nrm(ks[3], (DEPTH, N_ADA * D_MODEL), 0.01),
        "norm_ffn1": 1.0 + nrm(ks[4], (DEPTH, D_MODEL), 0.02),
        "w_ffn1_in": nrm(ks[5], (DEPTH, D_MODEL, 2 * D_FF), D_MODEL ** -0.5),
        "w_ffn1_out": nrm(ks[6], (DEPTH, D_FF, D_MODEL), D_FF ** -0.5),
        "norm_mix": 1.0 + nrm(ks[7], (DEPTH, D_MODEL), 0.02),
        "w_in": nrm(ks[8], (DEPTH, D_MODEL, IN_COLS), D_MODEL ** -0.5),
        "conv_w": nrm(ks[9], (DEPTH, SSD_CONV, SSD_CONV_DIM), SSD_CONV ** -0.5),
        "conv_b": nrm(ks[10], (DEPTH, SSD_CONV_DIM), 0.01),
        "dt_bias": dt_ssd + jnp.log(-jnp.expm1(-dt_ssd)),
        "a_log": jnp.log(jax.random.uniform(ks[12], (DEPTH, SSD_HEADS), f32, 1.0, 16.0)),
        "d_ssd": 1.0 + nrm(ks[13], (DEPTH, SSD_HEADS), 0.02),
        "ssd_norm_w": 1.0 + nrm(ks[14], (DEPTH, SSD_D_INNER), 0.02),
        "w_a_proj": nrm(ks[15], (DEPTH, SSD_D_INNER, D_MODEL), SSD_D_INNER ** -0.5),
        "s5_lambda_re": -0.5 + nrm(ks[17], (DEPTH, S5_GROUPS, S5_STATE), 0.01),
        "s5_lambda_im": lam_im,
        "s5_b_re": nrm(ks[18], (DEPTH, S5_GROUPS, S5_STATE, S5_GROUP_SIZE), (2 * S5_GROUP_SIZE) ** -0.5),
        "s5_b_im": nrm(ks[19], (DEPTH, S5_GROUPS, S5_STATE, S5_GROUP_SIZE), (2 * S5_GROUP_SIZE) ** -0.5),
        "s5_c_re": nrm(ks[20], (DEPTH, S5_GROUPS, S5_GROUP_SIZE, S5_STATE), (2 * S5_STATE) ** -0.5),
        "s5_c_im": nrm(ks[21], (DEPTH, S5_GROUPS, S5_GROUP_SIZE, S5_STATE), (2 * S5_STATE) ** -0.5),
        "s5_d": nrm(ks[22], (DEPTH, S5_GROUPS, S5_GROUP_SIZE), 1.0),
        "s5_log_dt": jax.random.uniform(ks[23], (DEPTH, S5_GROUPS), f32, math.log(1e-3), math.log(1e-1)),
        "w_b_glu": nrm(ks[24], (DEPTH, S5_WIDTH, 2 * D_MODEL), S5_WIDTH ** -0.5),
        "w_out": nrm(ks[25], (DEPTH, D_MODEL, D_MODEL), D_MODEL ** -0.5),
        "norm_ffn2": 1.0 + nrm(ks[26], (DEPTH, D_MODEL), 0.02),
        "w_ffn2_in": nrm(ks[27], (DEPTH, D_MODEL, 2 * D_FF), D_MODEL ** -0.5),
        "w_ffn2_out": nrm(ks[28], (DEPTH, D_FF, D_MODEL), D_FF ** -0.5),
        "norm_final": 1.0 + nrm(ks[29], (D_MODEL,), 0.02),
    }

def reference(x, c, w_ada, b_ada, norm_ffn1, w_ffn1_in, w_ffn1_out, norm_mix, w_in,
              conv_w, conv_b, dt_bias, a_log, d_ssd, ssd_norm_w, w_a_proj,
              s5_lambda_re, s5_lambda_im, s5_b_re, s5_b_im, s5_c_re, s5_c_im, s5_d, s5_log_dt,
              w_b_glu, w_out, norm_ffn2, w_ffn2_in, w_ffn2_out, norm_final):
    c_act = jax.nn.silu(c)
    for l in range(DEPTH):
        mods = (c_act @ w_ada[l] + b_ada[l])[:, None, :]
        (sh1, sc1, g1, sh2, sc2, g2, sh3, sc3, g3) = jnp.split(mods, N_ADA, axis=-1)

        h = modulate(x, norm_ffn1[l], sh1, sc1)
        x = x + 0.5 * g1 * swiglu(h, w_ffn1_in[l], w_ffn1_out[l])

        h = modulate(x, norm_mix[l], sh2, sc2)
        proj = h @ w_in[l]
        z, xbc, dt_raw, u, gates = jnp.split(proj, [OFF_XBC, OFF_DT, OFF_U, OFF_GATES], axis=-1)
        gate_a, gate_b = jnp.split(gates, 2, axis=-1)

        y_a = ssd_mixer(xbc, z, dt_raw, conv_w[l], conv_b[l], dt_bias[l], a_log[l], d_ssd[l], ssd_norm_w[l])
        p_a = y_a @ w_a_proj[l]

        y_b = s5_mixer(u, s5_lambda_re[l], s5_lambda_im[l], s5_b_re[l], s5_b_im[l],
                       s5_c_re[l], s5_c_im[l], s5_d[l], s5_log_dt[l])
        glu_a, glu_g = jnp.split(jax.nn.gelu(y_b) @ w_b_glu[l], 2, axis=-1)
        p_b = glu_a * jax.nn.sigmoid(glu_g)

        merged = jax.nn.sigmoid(gate_a) * p_a + jax.nn.sigmoid(gate_b) * p_b
        x = x + g2 * (merged @ w_out[l])

        h = modulate(x, norm_ffn2[l], sh3, sc3)
        x = x + 0.5 * g3 * swiglu(h, w_ffn2_in[l], w_ffn2_out[l])
    return rms_norm(x, norm_final)


_drawn_inputs = setup_inputs


def setup_inputs(seed=0):
    import zlib

    import numpy as np

    out = dict(_drawn_inputs(seed))
    spreads = {}
    factors = {'b_ada': 4.291,
     'norm_ffn1': 6.513,
     'norm_mix': 20.365,
     'conv_b': 64.0,
     'd_ssd': 200.0,
     'ssd_norm_w': 181.449,
     's5_lambda_re': 64.0,
     's5_lambda_im': 37.272,
     's5_b_re': 49.416,
     's5_b_im': 58.712,
     's5_c_re': 53.776,
     's5_c_im': 57.12,
     's5_log_dt': 49.888,
     'norm_ffn2': 31.13,
     'norm_final': 21.848}
    for name, (base, spread) in spreads.items():
        noise = np.random.default_rng([zlib.crc32(name.encode()), seed]).standard_normal(out[name].shape)
        drawn = base * np.exp(spread * noise) if base else spread * noise
        out[name] = __import__('jax').numpy.asarray(drawn.astype(out[name].dtype))
    for name, factor in factors.items():
        out[name] = (out[name] * factor).astype(out[name].dtype)
    return out
```

```python
from contextlib import ExitStack

import concourse.bass as bass
from concourse import mybir

F32 = mybir.dt.float32
F32R = mybir.dt.float32r
ACT = mybir.ActivationFunctionType
ALU = mybir.AluOpType

P = 128
D = 2048
S = 256
FF = 5504
NT = D // P
FT = FF // P
HEADS, HD, GROUPS, NST = 32, 64, 4, 128
HPG = HEADS // GROUPS
CONVD = D + 2 * GROUPS * NST
CT = CONVD // P
KW = 4
OFF_XBC = D
OFF_DT = OFF_XBC + CONVD
OFF_U = OFF_DT + HEADS
U = 1024
UT = U // P
S5G, S5I, S5P = 64, 16, 64
ST = S5G * S5P // P
OFF_GATES = OFF_U + U
EPS = 1e-6
COLS = 512
RING = 4
SPLIT = 2
FF1 = 20
TWO_PI = 6.283185307179586
PI_A, PI_B = 6.28125, 0.0019350051879882812
PI_C = TWO_PI - PI_A - PI_B
ROUND = 1.5 * 2.0 ** 23
PI_IN = 3.1415925


class Phase:

    def __init__(self, name, weight, col, k_tiles, bodies, evac, moving, ada=False, pair=0, row=0,
                 narrow=False, start=0, gate=None, last=False, step=COLS):
        self.name, self.weight, self.col, self.bodies, self.evac = name, weight, col, bodies, evac
        self.moving, self.ada, self.pair, self.row, self.narrow = moving, ada, pair, row, narrow
        self.start, self.gate, self.last, self.step = start, gate, last, step
        n = 6 if k_tiles > 16 else (k_tiles + 3) // 4
        self.chunks = [4] * n
        if k_tiles == 20:
            self.chunks = [4, 4, 3, 3, 3, 3]
        elif k_tiles == 23:
            self.chunks = [4, 4, 4, 4, 4, 3]
        assert sum(self.chunks) == k_tiles
        self.slabs = n
        self.stream = [("w", 0, s) for s in range(n)]
        for s in range(n):
            self.stream.append(("w", 1, s))
            if ada and s < 4:
                self.stream.append(("ada", 0, s))
        assert len(self.stream) % RING == 0 and n % SPLIT == 0


def plan():
    def ffn(n, gate):
        win, wout = f"w_ffn{n}_in", f"w_ffn{n}_out"
        ada = n == 1
        return [
            Phase("in", win, 0, NT, FF1 // 4, "pair", "h", ada, pair=FF),
            Phase("out", wout, 0, FF1, 2, "resid", "ff", ada, gate=gate),
            Phase("in", win, FF1 * P, NT, (FT - FF1) // 4, "pair", "h", ada, pair=FF),
            Phase("in", win, (FT - 3) * P, NT, 1, "pair", "h", False, pair=FF, start=(FT - 3 - FF1) // 2, narrow=True),
            Phase("out", wout, 0, FT - FF1, 2, "resid", "ff", ada, gate=gate, row=FF1 * P, last=(n == 2)),
        ]

    return (
        [("prologue", None), ("norm", 0)] + [("gemm", p) for p in ffn(1, 0)] + [("norm", 1)]
        + [("gemm", Phase("xbc", "w_in", OFF_XBC, NT, 3, "conv", "h", True)),
           ("gemm", Phase("u", "w_in", OFF_U, NT, 1, "copy", "h", True)),
           ("gemm", Phase("z", "w_in", 0, NT, 2, "silu", "h", True)),
           ("ssd", None), ("s5", None),
           ("gemm", Phase("gate_a", "w_in", OFF_GATES, NT, 2, "sig_a", "h", True)),
           ("gemm", Phase("gate_b", "w_in", OFF_GATES + D, NT, 2, "sig_b", "h", True)),
           ("split", None),
           ("gemm", Phase("a_proj", "w_a_proj", 0, NT, 2, "mul_a", "h", True)),
           ("gemm", Phase("b_glu", "w_b_glu", 0, U // P, 4, "glu", "yb", False, pair=D)),
           ("gemm", Phase("w_out", "w_out", 0, NT, 2, "resid", "h", True, gate=1)),
           ("norm", 2)] + [("gemm", p) for p in ffn(2, 2)] + [("final", None)]
    )


class Run:

    def __init__(self):
        self.n = self.m = self.q = self.c = self.p = self.g = 0


def build(nc, a):
    steps = plan()
    with ExitStack() as ctx:
        small_base = [0]
        arena = ctx.enter_context(nc.sbuf_tensor("arena", [P, 53120], F32))
        base = nc.sbuf_base - 53120 * 4

        def at(name, offset, shape, dt=F32):
            size = 4
            for s in shape[1:]:
                size *= s
            assert offset + size <= 53120 * 4, (name, offset + size)
            return nc.alloc_sbuf_tensor_at(name, shape, dt, offset=base + offset)

        def small(name, shape, dt=F32):
            size = 4
            for s in shape[1:]:
                size *= s
            size = (size + 31) // 32 * 32
            t = at(name, 200 * K + small_base[0], shape, dt)
            small_base[0] += size
            return t

        K = 1024
        xT = at("xT", 0, [P, NT, S])
        hs = at("hs", 16 * K, [P, NT, 2, S], F32R)
        raw = at("raw", 48 * K, [P, RING, 4, COLS])
        whi = at("whi", 80 * K, [P, SPLIT, 4, COLS], F32R)
        wlo = at("wlo", 96 * K, [P, SPLIT, 4, COLS], F32R)
        R = 112 * K
        ffs = at("ffs", R, [P, FT - FF1, 2, S], F32R)
        xw = at("xw", R + 48 * K, [P, NT, S])
        xbc = at("xbc", R, [P, CT, S])
        ub = at("ub", R + 24 * K, [P, UT, S])
        zb = at("zb", R + 32 * K, [P, NT, S])
        ga = at("ga", R + 32 * K, [P, NT, S])
        gb = at("gb", R + 48 * K, [P, NT, S])
        ybs = at("ybs", R + 64 * K, [P, UT, 2, S], F32R)
        wdt = at("wdt", R + 64 * K, [P, NT, HEADS])
        wdth = at("wdth", R + 66 * K, [P, NT, HEADS], F32R)
        wdtl = at("wdtl", R + 68 * K, [P, NT, HEADS], F32R)
        W = R + 48 * K
        xst = at("xst", W, [P, 4, S])
        bst = at("bst", W + 4 * K, [P, S])
        cst = at("cst", W + 5 * K, [P, S])
        xdt = at("xdt", W + 6 * K, [P, 2, HPG * HD])
        xde = at("xde", W + 10 * K, [P, HPG * HD])
        prev = at("prev", W + 12 * K, [P, HPG * HD])
        yof = at("yof", W + 14 * K, [P, HPG * HD])
        E = [at(f"E{c}", W + (16 + 4 * c) * K, [P, HPG, P]) for c in range(2)]
        ytok = at("ytok", W + 24 * K, [P, 2, HPG * HD])
        cbm = at("cbm", W + 28 * K, [P, 2, P])
        btok = at("btok", W + 29 * K, [P, P])
        t1 = at("t1", W, [P, 4, S])
        t2 = at("t2", W + 4 * K, [P, 4, S])
        wr = at("wr", W + 8 * K, [P, 4, S])
        wi = at("wi", W + 12 * K, [P, 4, S])
        tc = at("tc", W + 16 * K, [P, 4, S])
        ts = at("ts", W + 20 * K, [P, 4, S])
        ctb = at("ctb", W + 24 * K, [P, 2, 4, P])
        btb = at("btb", W + 28 * K, [P, 2, 4, P])
        bblk = at("bblk", W, [P, 2, 4, 8, S5I])
        cblk = at("cblk", W + 4 * K, [P, 2, 8, S5P])
        Z = R + 32 * K
        bbar = at("bbar", Z, [P, 2, ST, S5I])
        cnat = at("cnat", Z + 4 * K, [P, 2, UT, S5P])
        rot = at("rot", Z + 8 * K, [P, 4, ST, 16])
        bnat = at("bnat", W, [P, 2, ST, S5I])
        q1 = at("q1", W + 4 * K, [P, ST, S5I])
        q2 = at("q2", W + 6 * K, [P, ST, S5I])
        sp = at("sp", W + 8 * K, [P, 24, ST])
        T = R + 80 * K
        sil = at("sil", T, [P, 2, S])
        prod = at("prod", T + 2 * K, [P, 2, S])
        acc = at("acc", T + 4 * K, [P, COLS])
        var = at("var", T + 6 * K, [P, S])
        rs = at("rs", T + 7 * K, [P, S])
        xin = at("xin", R, [P, 2, D])
        rows = at("rows", R + 16 * K, [P, 4, P])
        ones_i = at("ones_i", R + 18 * K, [P, P])
        xout = at("xout", R, [P, 2, D])

        mods = small("mods", [P, 9 * NT])
        gm = small("gm", [P, 3, NT])
        hg = small("hg", [P, 3, NT])
        pv = small("pv", [P, 4, P])
        ident = small("ident", [P, P])
        ones = small("ones", [P, P])
        tri = small("tri", [P, P])
        cact = small("cact", [P, NT])
        maskb = small("maskb", [P, 4, 8])
        maskc = small("maskc", [P, 2, 8])
        dcol = small("dcol", [P, NT])
        mag = small("mag", [P, ST])
        hb = small("hb", [P, 4, HEADS])
        ldt = small("ldt", [P, S5G])
        dtv = small("dtv", [P, 2, HEADS])
        da = small("da", [P, 2, HEADS])
        cs = small("cs", [P, 2, HEADS])
        wend = small("wend", [P, 2, HEADS])
        ecs = small("ecs", [P, 2, HEADS])
        dta = small("dta", [P, 2, HEADS])
        dtb = small("dtb", [P, 2, HEADS])
        das = small("das", [P, 2, HPG])
        css = small("css", [P, 2, HPG])
        assert small_base[0] <= 53120 * 4 - 200 * K

        gps = ctx.enter_context(nc.psum_tensor("gps", [P, 2, 4, S], F32))
        mps = ctx.enter_context(nc.psum_tensor("mps", [P, 4, 512], F32))

        C_IN, N_FFN1, N_MIX, N_FFN2, N_FIN, N_SSD, CONV_B, S5_D = (pv[:, 0, i:i + w] for i, w in (
            (0, 16), (16, 16), (32, 16), (48, 16), (64, 16), (80, 16), (96, 24), (120, 8)))
        CONV_W = pv[:, 1, 0:96]
        LAM_RE = pv[:, 1, 96:128]
        B_ADA = pv[:, 2:4, :].rearrange("p a b -> p (a b)")[:, 0:9 * NT]
        LAM_IM = pv[:, 3, 16:48]
        NORMS = [N_FFN1, N_MIX, N_FFN2]

        sems = {}

        def sem(name):
            if name not in sems:
                sems[name] = ctx.enter_context(nc.semaphore(name))
            return sems[name]

        def landed(slot):
            return sem(f"slab_landed{slot}")

        def psum_free(b):
            return sem(f"outputs_read{b}")

        raw_used, hi_ready, slab_done = sem("slab_used"), sem("hi_ready"), sem("slab_multiplied")
        block = ctx.enter_context(nc.Block())

        def mm(pe, out, lhsT, rhs, start, stop):
            return pe.matmul(out, lhsT, rhs, start=start, stop=stop, skip_group_check=True)

        @block.sync
        def _(sync):
            r = Run()
            x_t = a["x"][0].rearrange("(c p) d -> p c d", p=P)
            sync.dma_start(xin[:, :, :], x_t).then_inc(sem("x_in"), 16)

            def vec(name, row, at_row, tile=0):
                v = a[name].rearrange("(t p) -> t p", p=P)
                sync.dma_start(rows[at_row:at_row + row, tile, :], v).then_inc(sem("rows_in"), 16)

            vec_list = [("c", a["c"][0], 0, 0), ("n1", a["norm_ffn1"][0], 16, 0), ("nm", a["norm_mix"][0], 32, 0),
                        ("n2", a["norm_ffn2"][0], 48, 0), ("nf", a["norm_final"], 64, 0),
                        ("sn", a["ssd_norm_w"][0], 80, 0), ("cb", a["conv_b"][0], 96, 0),
                        ("sd", a["s5_d"][0].rearrange("g i -> (g i)"), 120, 0),
                        ("cw", a["conv_w"][0].rearrange("k c -> (k c)"), 0, 1),
                        ("lr", a["s5_lambda_re"][0].rearrange("g p -> (g p)"), 96, 1),
                        ("b1", a["b_ada"][0][0:P * P], 0, 2), ("b2", a["b_ada"][0][P * P:], 0, 3),
                        ("li", a["s5_lambda_im"][0].rearrange("g p -> (g p)"), 16, 3),
                        ("pad", a["b_ada"][0][0:80 * P], 48, 3)]
            for _, v, row, tile in vec_list:
                v = v.rearrange("(t p) -> t p", p=P)
                sync.dma_start(rows[row:row + v.shape[0], tile, :], v).then_inc(sem("rows_in"), 16)
            for j, name in enumerate(("a_log", "dt_bias", "d_ssd")):
                sync.dma_start(hb[:, j, :], a[name][0:1, :].broadcast_to([P, HEADS])).then_inc(sem("heads_in"), 16)
            sync.dma_start(ldt[:, :], a["s5_log_dt"][0:1, :].broadcast_to([P, S5G])).then_inc(sem("heads_in"), 16)

            def slab(n, pos, src_parts):
                if not (isinstance(n, int) and n < RING):
                    sync.wait_ge(raw_used, n - (RING - 1))
                for dst, src in src_parts:
                    sync.dma_start(dst, src).then_inc(landed(pos % RING), 32 // len(src_parts))

            ada = a["w_ada"][0].rearrange("(k p) n -> p k n", p=P)

            def ada_slab(n, pos, c, s):
                slab(n, pos, [(raw[:, pos % RING, :, :], ada[:, 4 * s:4 * s + 4, bass.ds(c * COLS, COLS)])])

            for kind, ph in steps:
                if kind == "prologue":
                    for s in range(4):
                        ada_slab(s, s, 0, s)
                    with sync.Fori(1, 8) as i:
                        for s in range(4):
                            ada_slab(i * 4 + s, s, i, s)
                    r.n, r.c = 32, 8
                elif kind == "gemm":
                    w = a[ph.weight][0][ph.row:ph.row + sum(ph.chunks) * P, :].rearrange("(k p) n -> p k n", p=P)
                    per = len(ph.stream)

                    def body(i, narrow=False):
                        for pos, (what, g, s) in enumerate(ph.stream):
                            n = r.n + i * per + pos
                            if what == "ada":
                                ada_slab(n, pos, r.c + i, s)
                                continue
                            k0, kc = sum(ph.chunks[:s]), ph.chunks[s]
                            dst = raw[:, pos % RING, 0:kc, :]
                            if ph.pair:
                                width = P if (ph.narrow and g == 1) else COLS // 2
                                col = ph.col + (i * 2 + g) * (COLS // 2)
                                parts = [(dst[:, :, h * COLS // 2:h * COLS // 2 + width],
                                          w[:, k0:k0 + kc, bass.ds(col + h * ph.pair, width)]) for h in range(2)]
                            else:
                                parts = [(dst, w[:, k0:k0 + kc, bass.ds(ph.col + (i * 2 + g) * COLS, COLS)])]
                            slab(n, pos, parts)

                    if ph.bodies > 1:
                        with sync.Fori(0, ph.bodies) as i:
                            body(i)
                    else:
                        body(0)
                    r.n += per * ph.bodies
                    r.c += ph.ada * ph.bodies
                elif kind == "norm" and ph == 1:
                    sync.dma_start(wdt[:, :, :], a["w_in"][0].rearrange("(k p) n -> p k n", p=P)[:, :, OFF_DT:OFF_U]
                                   ).then_inc(sem("wdt_in"), 16)
                elif kind == "final":
                    sync.wait_ge(sem("out_ready"), 1)
                    sync.dma_start(a["out"][0].rearrange("(c p) d -> p c d", p=P), xout[:, :, :]
                                   ).then_inc(sem("out_written"), 16)
                    sync.wait_ge(sem("out_written"), 16)

        @block.gpsimd
        def _(pool):
            def mask(t, pattern, base, mult, op, fill):
                pool.affine_select(out=t, in_=t, compare_op=op, fill=fill, base=base, pattern=pattern,
                                   channel_multiplier=mult).then_inc(sem("mask_step"), 1)

            pool.memset(ident[:, :], 0.0).then_inc(sem("mask_step"), 1)
            pool.memset(ones[:, :], 1.0).then_inc(sem("mask_step"), 1)
            pool.memset(tri[:, :], 1.0).then_inc(sem("mask_step"), 1)
            pool.memset(maskb[:, :, :], 0.0).then_inc(sem("mask_step"), 1)
            pool.memset(maskc[:, :, :], 1.0).then_inc(sem("mask_step"), 1)
            pool.wait_ge(sem("mask_step"), 5)
            mask(ident[:, :], [[-1, P]], 0, 1, ALU.not_equal, 1.0)
            mask(tri[:, :], [[1, P]], 0, -1, ALU.is_ge, 0.0)
            mask(maskc[:, 0, :], [[-16, 8]], 0, 1, ALU.is_ge, 0.0)
            pool.wait_ge(sem("mask_step"), 8)
            mask(maskc[:, 0, :], [[16, 8]], 15, -1, ALU.is_ge, 0.0)
            pool.wait_ge(sem("mask_step"), 9)
            for half in range(2):
                pool.memset(maskc[64 * half:64 * half + 64, 1, :], 0.0).then_inc(sem("mask_step"), 1)
            for j in range(4):
                for half in range(2):
                    g = 2 * j + half
                    pool.memset(maskb[64 * half:64 * half + 64, j, g:g + 1], 1.0).then_inc(sem("mask_step"), 1)
            pool.wait_ge(sem("mask_step"), 19)
            pool.tensor_scalar(maskc[:, 1, :], maskc[:, 0, :], -1.0, None, ALU.mult).then_inc(sem("masks"), 1)

            pool.wait_ge(sem("ssd_group_done"), GROUPS + 1)
            for j, name in enumerate(("s5_b_re", "s5_b_im")):
                pool.dma_start(bnat[:, j, :, :], a[name][0].rearrange("(t g) p i -> (g p) t i", g=2)
                               ).then_inc(sem("s5_in"), 16)
            for j, name in enumerate(("s5_c_re", "s5_c_im")):
                pool.dma_start(cnat[:, j, :, :], a[name][0].rearrange("(t g) i p -> (g i) t p", g=8)
                               ).then_inc(sem("s5_in"), 16)

            pool.wait_ge(sem("s5_constants"), 1)
            with pool.Fori(0, UT) as i:
                pool.wait_ge(sem("s5_tile_done"), i + 1)
                pool.wait_ge(sem("s5_turned"), i + 1)
                hc, hn, lc, ln = (rot[:, w, bass.ds(4 * i, 4), :] for w in range(4))
                big = [v.unsqueeze(3).broadcast_to([P, 4, 16, 16]) for v in (hc, hn)]
                few = [v.unsqueeze(2).broadcast_to([P, 4, 16, 16]) for v in (lc, ln)]
                v4 = [t[:, :, :].rearrange("p s (j k) -> p s j k", j=16) for t in (tc, ts, t1, t2)]
                pool.tensor_tensor(v4[0], big[0], few[0], ALU.mult)
                pool.tensor_tensor(v4[2], big[1], few[1], ALU.mult)
                pool.tensor_tensor(v4[1], big[1], few[0], ALU.mult)
                pool.tensor_tensor(v4[3], big[0], few[1], ALU.mult).then_inc(sem("rot_products"), 1)
                pool.wait_ge(sem("rot_products"), i + 1)
                pool.tensor_tensor(tc[:, :, :], tc[:, :, :], t1[:, :, :], ALU.subtract)
                pool.tensor_tensor(ts[:, :, :], ts[:, :, :], t2[:, :, :], ALU.add).then_inc(sem("rot_ready"), 1)

        @block.scalar
        def _(act):
            r = Run()

            def hi(lap, pos, m, mpos):
                act.wait_ge(landed(pos % RING), lap * 32 + 32)
                if not (isinstance(m, int) and m < SPLIT):
                    act.wait_ge(slab_done, m - (SPLIT - 1))
                act.activation(whi[:, mpos % SPLIT, :, :], raw[:, pos % RING, :, :], ACT.Copy).then_inc(hi_ready, 1)

            act.wait_ge(sem("rows_turned"), 1)
            act.activation(pv[:, :, :].rearrange("p a b -> p (a b)"), mps[:, 0, :], ACT.Copy).then_inc(sem("vectors"), 1)
            act.wait_ge(sem("vectors"), 1)
            act.activation(cact[:, :], C_IN, ACT.Silu).then_inc(sem("c_act"), 1)
            for t in range(4):
                act.wait_ge(sem("x_turned"), t + 1)
                act.activation(xT[:, 4 * t:4 * t + 4, :], gps[:, t % 2, :, :], ACT.Copy).then_inc(sem("x_ready"), 1)

            weights = [ph for kind, ph in steps if kind == "gemm"]
            starts, n, m = {}, 32, 0
            for ph in weights:
                starts[id(ph)] = (n, m)
                n += len(ph.stream) * ph.bodies
                m += 2 * ph.slabs * ph.bodies

            def first_two(ph, i=None):
                n0, m0 = starts[id(ph)]
                per = len(ph.stream)
                for s in range(2):
                    if i is None:
                        hi(n0 // RING, s, m0 + s, s)
                    else:
                        hi(n0 // RING + (i + 1) * (per // RING), s, m0 + (i + 1) * 2 * ph.slabs + s, s)

            def evacuate(ph, i, g, m_end, q):
                b = g
                act.wait_ge(slab_done, m_end)
                out = gps[:, b, :, :]
                if ph.evac == "pair":
                    act.wait_ge(sem("prod_free"), r.p + i * 2 + g + 1)
                    act.activation(sil[:, :, :], out[:, 0:2, :], ACT.Silu).then_inc(sem("silu_ready"), 1)
                    act.wait_ge(psum_free(b), q)
                    f = ph.start + i * 2 + g
                    k = 2
                    if ph.narrow and g == 1:
                        k = 1
                    act.activation(ffs[:, bass.ds(2 * f, k), 0, :], prod[:, 0:k, :], ACT.Copy).then_inc(sem("ff_hi"), 1)
                elif ph.evac == "conv":
                    act.wait_ge(psum_free(b), q)
                    t = xbc[:, bass.ds(8 * i + 4 * g, 4), :]
                    act.activation(t, t, ACT.Silu).then_inc(sem("xbc_ready"), 1)
                elif ph.evac in ("copy", "silu", "sig_a", "sig_b"):
                    dst, f = {"copy": (ub, ACT.Copy), "silu": (zb, ACT.Silu), "sig_a": (ga, ACT.Sigmoid),
                              "sig_b": (gb, ACT.Sigmoid)}[ph.evac]
                    act.activation(dst[:, bass.ds(8 * i + 4 * g, 4), :], out, f).then_inc(psum_free(b), 1)
                elif ph.evac == "glu":
                    act.wait_ge(sem("prod_free"), r.p + i * 2 + g + 1)
                    act.activation(sil[:, :, :], out[:, 2:4, :], ACT.Sigmoid).then_inc(sem("silu_ready"), 1)
                    act.wait_ge(sem("merged"), i * 2 + g + 1)
                    act.activation(hs[:, bass.ds(4 * i + 2 * g, 2), 0, :], prod[:, :, :], ACT.Copy
                                   ).then_inc(sem("ff_hi"), 1)

            def gemm(ph, following):
                n0, m0 = starts[id(ph)]
                per, mper = len(ph.stream), 2 * ph.slabs

                def body(i, nxt):
                    for g in range(2):
                        for pos, (what, gg, s) in enumerate(ph.stream):
                            if what == "w" and gg == g and s >= 2:
                                mp = gg * ph.slabs + s
                                hi(n0 // RING + i * (per // RING) + pos // RING, pos, m0 + i * mper + mp, mp)
                        if g == 0:
                            for pos, (what, gg, s) in enumerate(ph.stream):
                                if what == "w" and gg == 1 and s < 2:
                                    mp = ph.slabs + s
                                    hi(n0 // RING + i * (per // RING) + pos // RING, pos, m0 + i * mper + mp, mp)
                        elif nxt == "loop":
                            first_two(ph, i)
                        elif nxt is not None:
                            first_two(nxt)
                        evacuate(ph, i, g, m0 + i * mper + (g + 1) * ph.slabs, r.q + i + 1)

                if ph.bodies > 1:
                    with act.Fori(0, ph.bodies - 1) as i:
                        body(i, "loop")
                body(ph.bodies - 1, following)
                r.q += ph.bodies
                if ph.evac in ("pair", "glu"):
                    r.p += 2 * ph.bodies

            def norm(k, last=False):
                act.wait_ge(sem("x_ready"), 4)
                for b in range(2):
                    if r.q:
                        act.wait_ge(psum_free(b), r.q)
                if k:
                    act.wait_ge(sem("h_lo"), 4 * k)
                    act.wait_ge(slab_done, r.m)
                for t in range(4):
                    act.activation(xw[:, 4 * t:4 * t + 4, :], xT[:, 4 * t:4 * t + 4, :], ACT.Square
                                   ).then_inc(sem("squares"), 1)
                act.wait_ge(sem("variance"), k + 1)
                act.activation(rs[:, :], var[:, :], ACT.Sqrt).then_inc(sem("deviation"), 1)
                if last:
                    return
                for t in range(4):
                    act.wait_ge(sem("h_ready"), 4 * k + t + 1)
                    act.activation(hs[:, 4 * t:4 * t + 4, 0, :], xw[:, 4 * t:4 * t + 4, :], ACT.Copy
                                   ).then_inc(sem("h_hi"), 1)

            def ssd():
                for b in range(2):
                    act.wait_ge(psum_free(b), r.q)
                act.wait_ge(sem("xbc_ready"), 6)
                act.wait_ge(sem("wdt_in"), 16)
                act.activation(wdth[:, :, :], wdt[:, :, :], ACT.Copy).then_inc(sem("wdt_hi"), 1)
                act.activation(hb[:, 3, :], hb[:, 0, :], ACT.Exp).then_inc(sem("a_exp"), 1)
                act.wait_ge(sem("dt_abs"), 1)
                act.activation(dta[:, :, :], dta[:, :, :], ACT.Exp, scale=-1.0).then_inc(sem("dt_exp"), 1)
                act.wait_ge(sem("dt_one_more"), 1)
                act.activation(dtv[:, :, :], dtb[:, :, :], ACT.Ln).then_inc(sem("dt_ln"), 1)
                act.wait_ge(sem("wend_arg"), 1)
                act.activation(wend[:, :, :], wend[:, :, :], ACT.Exp)
                act.activation(ecs[:, :, :], cs[:, :, :], ACT.Exp).then_inc(sem("decays"), 1)
                with act.Fori(0, GROUPS) as i:
                    one = i + 1
                    act.wait_ge(sem("ssd_group_done"), one)
                    act.activation(xst[:, :, :], xbc[:, bass.ds(4 * i, 4), :], ACT.Copy)
                    act.activation(bst[:, :], xbc[:, bass.ds(16 + i, 1), :].rearrange("p a s -> p (a s)"), ACT.Copy)
                    act.activation(cst[:, :], xbc[:, bass.ds(20 + i, 1), :].rearrange("p a s -> p (a s)"), ACT.Copy
                                   ).then_inc(sem("ssd_staged"), 1)
                    act.wait_ge(sem("b_and_cb"), one)
                    act.activation(btok[:, :], mps[:, 2, 0:P], ACT.Copy).then_inc(sem("b_tokens"), 1)
                    act.wait_ge(sem("state"), one)
                    act.activation(prev[:, :], mps[:, 3, :], ACT.Copy).then_inc(sem("state_kept"), 1)
                    for c in range(2):
                        act.wait_ge(sem(f"seg_in{c}"), one)
                        act.activation(E[c][:, :, :], E[c][:, :, :], ACT.Exp).then_inc(sem(f"seg_exp{c}"), 1)
                        if c == 0:
                            act.wait_ge(sem("y_diag0"), one)
                            act.activation(ytok[:, 0, :], mps[:, 2, :], ACT.Copy).then_inc(sem("y_tok0"), 1)
                    act.wait_ge(sem("y_gated"), one)
                    act.activation(E[0][:, :, :], E[1][:, :, :], ACT.Square).then_inc(sem("y_squares"), 1)
                    act.wait_ge(sem("y_var"), one)
                    act.activation(rs[:, :], var[:, :], ACT.Sqrt).then_inc(sem("y_dev"), 1)

            def s5():
                act.wait_ge(sem("ssd_group_done"), GROUPS + 1)
                act.wait_ge(sem("s5_logdt"), 1)
                act.activation(sp[:, 0, :], sp[:, 1, :], ACT.Exp).then_inc(sem("s5_dt"), 1)
                act.wait_ge(sem("s5_angle"), 1)
                act.activation(sp[:, 5, :], sp[:, 4, :], ACT.Tanh, scale=0.5)
                act.activation(sp[:, 6, :], sp[:, 3, :], ACT.Sin)
                act.activation(sp[:, 7, :], sp[:, 3, :], ACT.Sin, scale=0.5).then_inc(sem("s5_sines"), 1)
                act.activation(sp[:, 22, :], sp[:, 1, :], ACT.Copy).then_inc(sem("s5_tile_done"), 1)
                with act.Fori(0, UT) as i:
                    one = i + 1
                    act.wait_ge(sem("s5_tile_done"), one)
                    act.activation(sil[:, 0, :], ub[:, bass.ds(i, 1), :].rearrange("p a s -> p (a s)"), ACT.Copy
                                   ).then_inc(sem("u_staged"), 1)
                    act.wait_ge(sem("s5_turned"), one)
                    act.activation(btb[:, :, :, :].rearrange("p a b c -> p (a b c)"),
                                   mps[:, 0:2, :].rearrange("p a b -> p (a b)"), ACT.Copy)
                    act.activation(ctb[:, :, :, :].rearrange("p a b c -> p (a b c)"),
                                   mps[:, 2:4, :].rearrange("p a b -> p (a b)"), ACT.Copy).then_inc(sem("s5_mats"), 1)
                    act.wait_ge(sem("s5_y"), one)
                    act.activation(var[:, :], sil[:, 1, :], ACT.Gelu_apprx_tanh).then_inc(sem("s5_gelu"), 1)

            def split():
                for b in range(2):
                    act.wait_ge(psum_free(b), r.q)
                act.wait_ge(slab_done, r.m)
                act.wait_ge(sem("ssd_group_done"), GROUPS + 1)
                act.wait_ge(sem("s5_tile_done"), UT + 1)
                act.activation(hs[:, :, 0, :], xbc[:, 0:NT, :], ACT.Copy).then_inc(sem("y_hi"), 1)
                act.activation(ybs[:, :, 0, :], ub[:, :, :], ACT.Copy).then_inc(sem("y_hi"), 1)

            def final():
                norm(3, last=True)
                for t in range(4):
                    act.wait_ge(sem("y_turned"), 2 * t + 1)
                    act.activation(xout[:, 0, 512 * t:512 * t + 512], mps[:, 0, :], ACT.Copy).then_inc(sem("y_out"), 1)
                    act.wait_ge(sem("y_turned"), 2 * t + 2)
                    act.activation(xout[:, 1, 512 * t:512 * t + 512], mps[:, 1, :], ACT.Copy).then_inc(
                        sem("y_out") if t < 3 else sem("out_ready"), 1)

            todo = list(weights)
            for kind, ph in steps:
                if kind == "norm":
                    norm(ph)
                    if ph == 0:
                        first_two(todo[0])
                elif kind == "gemm":
                    todo.pop(0)
                    gemm(ph, todo[0] if todo else None)
                    r.m += 2 * ph.slabs * ph.bodies
                elif kind == "ssd":
                    ssd()
                elif kind == "s5":
                    s5()
                elif kind == "split":
                    split()
                elif kind == "final":
                    final()

        @block.vector
        def _(dve):
            r = Run()
            chain = [0]

            def link(ins):
                ins.then_inc(sem("vector_step"), 1)
                chain[0] += 1
                dve.wait_ge(sem("vector_step"), chain[0])

            def lo(lap, pos, m, mpos):
                dve.wait_ge(hi_ready, m + 1)
                dve.tensor_tensor(wlo[:, mpos % SPLIT, :, :], raw[:, pos % RING, :, :],
                                  whi[:, mpos % SPLIT, :, :].bitcast(F32), ALU.subtract).then_inc(raw_used, 1)

            def ada_slab(lap, pos, c, s):
                dve.wait_ge(landed(pos % RING), lap * 32 + 32)
                for k in range(4):
                    kk = 4 * s + k
                    w = raw[:, pos % RING, k, :]
                    if kk == 0:
                        ins = dve.tensor_scalar(acc[:, :], w, cact[:, 0:1], None, ALU.mult)
                    else:
                        if k:
                            dve.wait_ge(sem("ada_step"), c * 12 + 3 * s + k)
                        else:
                            dve.wait_ge(sem("ada_quarter"), c * 4 + s)
                        ins = dve.scalar_tensor_tensor(out=acc[:, :], in0=w, scalar=cact[:, kk:kk + 1], in1=acc[:, :],
                                                       op0=ALU.mult, op1=ALU.add)
                    if k < 3:
                        ins.then_inc(sem("ada_step"), 1)
                    else:
                        ins.then_inc(raw_used, 1)
                        dve.wait_ge(raw_used, lap * RING + pos % RING + 1)
                        dve.tensor_copy(css[0:1, 0, 0:1], cact[0:1, 0:1]).then_inc(sem("ada_quarter"), 1)

            def ada_end(c):
                dve.wait_ge(sem("ada_sum"), c + 1)
                dve.tensor_tensor(mods[:, bass.ds(4 * c, 4)], mps[:, 3, 0:4], B_ADA[:, bass.ds(4 * c, 4)], ALU.add
                                  ).then_inc(sem("ada_done"), 1)

            dve.wait_ge(sem("masks"), 1)
            dve.wait_ge(sem("c_act"), 1)
            dve.memset(prod[:, :, :], 0.0).then_inc(sem("prod_free"), 1)
            with dve.Fori(0, 8) as i:
                for s in range(4):
                    ada_slab(i, s, i, s)
                ada_end(i)
            r.c = 8

            weights = [ph for kind, ph in steps if kind == "gemm"]
            starts, n, m = {}, 32, 0
            for ph in weights:
                starts[id(ph)] = (n, m)
                n += len(ph.stream) * ph.bodies
                m += 2 * ph.slabs * ph.bodies

            def first_two(ph, i=None):
                n0, m0 = starts[id(ph)]
                per = len(ph.stream)
                for s in range(2):
                    if i is None:
                        lo(n0 // RING, s, m0 + s, s)
                    else:
                        lo(n0 // RING + (i + 1) * (per // RING), s, m0 + (i + 1) * 2 * ph.slabs + s, s)

            def evacuate(ph, i, g, m_end, q):
                b = g
                out = gps[:, b, :, :]
                if ph.evac == "pair":
                    p = r.p + i * 2 + g
                    dve.wait_ge(sem("silu_ready"), p + 1)
                    dve.tensor_tensor(prod[:, :, :], sil[:, :, :], out[:, 2:4, :], ALU.mult).then_inc(psum_free(b), 1)
                    dve.wait_ge(sem("ff_hi"), p + 1)
                    f = ph.start + i * 2 + g
                    k = 1 if ph.narrow and g == 1 else 2
                    dve.tensor_tensor(ffs[:, bass.ds(2 * f, k), 1, :], prod[:, 0:k, :],
                                      ffs[:, bass.ds(2 * f, k), 0, :].bitcast(F32), ALU.subtract
                                      ).then_inc(sem("prod_free"), 1)
                elif ph.evac == "resid":
                    dve.wait_ge(slab_done, m_end)
                    gate = hg[:, ph.gate, :]
                    for j in range(4):
                        t = 8 * i + 4 * g + j
                        xt = xT[:, bass.ds(t, 1), :].rearrange("p a s -> p (a s)")
                        ins = dve.scalar_tensor_tensor(out=xt, in0=out[:, j, :], scalar=gate[:, bass.ds(t, 1)],
                                                       in1=xt, op0=ALU.mult, op1=ALU.add)
                    ins.then_inc(psum_free(b), 1)
                elif ph.evac == "conv":
                    dve.wait_ge(slab_done, m_end)
                    for op in range(4 * KW):
                        lag, j = op // 4, op % 4
                        t = 8 * i + 4 * g + j
                        tap = CONV_W[:, bass.ds(CT * (KW - 1 - lag) + t, 1)]
                        dst = xbc[:, bass.ds(t, 1), :].rearrange("p a s -> p (a s)")
                        if lag == 0:
                            ins = dve.tensor_scalar(dst, out[:, j, :], tap, CONV_B[:, bass.ds(t, 1)],
                                                    ALU.mult, ALU.add)
                        else:
                            dve.wait_ge(sem("conv_step"), (2 * i + g) * 15 + op - 3)
                            ins = dve.scalar_tensor_tensor(out=dst[:, lag:S], in0=out[:, j, 0:S - lag], scalar=tap,
                                                           in1=dst[:, lag:S], op0=ALU.mult, op1=ALU.add)
                        ins.then_inc(sem("conv_step") if op < 15 else psum_free(b), 1)
                elif ph.evac == "mul_a":
                    dve.wait_ge(slab_done, m_end)
                    g_t = ga[:, bass.ds(8 * i + 4 * g, 4), :]
                    dve.tensor_tensor(g_t, out, g_t, ALU.mult).then_inc(psum_free(b), 1)
                elif ph.evac == "glu":
                    p = r.p + i * 2 + g
                    t = bass.ds(4 * i + 2 * g, 2)
                    dve.wait_ge(sem("silu_ready"), p + 1)
                    dve.tensor_tensor(prod[:, :, :], sil[:, :, :], out[:, 0:2, :], ALU.mult).then_inc(psum_free(b), 1)
                    dve.wait_ge(psum_free(b), q)
                    dve.tensor_tensor(prod[:, :, :], prod[:, :, :], gb[:, t, :], ALU.mult).then_inc(sem("p_b"), 1)
                    dve.wait_ge(sem("p_b"), i * 2 + g + 1)
                    dve.tensor_tensor(prod[:, :, :], prod[:, :, :], ga[:, t, :], ALU.add).then_inc(sem("merged"), 1)
                    dve.wait_ge(sem("ff_hi"), p + 1)
                    dve.tensor_tensor(hs[:, t, 1, :], prod[:, :, :], hs[:, t, 0, :].bitcast(F32), ALU.subtract
                                      ).then_inc(sem("prod_free"), 1)

            def gemm(ph, following):
                n0, m0 = starts[id(ph)]
                per, mper = len(ph.stream), 2 * ph.slabs
                for b in range(2):
                    if r.q:
                        dve.wait_ge(psum_free(b), r.q)
                if r.p:
                    dve.wait_ge(sem("prod_free"), r.p + 1)
                if ph.evac == "resid" and ph.gate is not None:
                    dve.wait_ge(sem("ada_done"), r.c)

                def body(i, nxt):
                    for g in range(2):
                        for pos, (what, gg, s) in enumerate(ph.stream):
                            lap = n0 // RING + i * (per // RING) + pos // RING
                            first = gg == 1 and s < 2
                            mine = (gg == 0 and s >= 2 or first) if g == 0 else (gg == 1 and s >= 2)
                            if what == "ada" and (s < 2) == (g == 0):
                                ada_slab(lap, pos, r.c + i, s)
                            elif what == "w" and mine:
                                mp = gg * ph.slabs + s
                                lo(lap, pos, m0 + i * mper + mp, mp)
                        if g == 1:
                            if nxt == "loop":
                                first_two(ph, i)
                            elif nxt is not None:
                                first_two(nxt)
                        evacuate(ph, i, g, m0 + i * mper + (g + 1) * ph.slabs, r.q + i + 1)
                    if ph.ada:
                        ada_end(r.c + i)

                if ph.bodies > 1:
                    with dve.Fori(0, ph.bodies - 1) as i:
                        body(i, "loop")
                body(ph.bodies - 1, following)
                r.q += ph.bodies
                r.c += ph.ada * ph.bodies
                if ph.evac in ("pair", "glu"):
                    r.p += 2 * ph.bodies

            def gates(k):
                link(dve.tensor_scalar(hg[:, k, :], mods[:, 16 * (3 * k + 2):16 * (3 * k + 3)],
                                       1.0 if k == 1 else 0.5, None, ALU.mult))

            def norm(k, last=False):
                dve.wait_ge(sem("ada_done"), r.c)
                for b in range(2):
                    if r.q:
                        dve.wait_ge(psum_free(b), r.q)
                if not last:
                    link(dve.tensor_scalar(gm[:, k, :], mods[:, 16 * (3 * k + 1):16 * (3 * k + 2)], 1.0, None, ALU.add))
                    link(dve.tensor_tensor(gm[:, k, :], gm[:, k, :], NORMS[k], ALU.mult))
                dve.wait_ge(sem("sum_squares"), k + 1)
                dve.tensor_scalar(var[:, :], mps[:, 2, 0:S], 1.0 / D, EPS, ALU.mult, ALU.add
                                  ).then_inc(sem("variance"), 1)
                dve.wait_ge(sem("deviation"), k + 1)
                link(dve.reciprocal(rs[:, :], rs[:, :]))
                for t in range(4):
                    q = xw[:, 4 * t:4 * t + 4, :]
                    link(dve.tensor_tensor(q, xT[:, 4 * t:4 * t + 4, :],
                                           rs[:, :].unsqueeze(1).broadcast_to([P, 4, S]), ALU.mult))
                    for j in range(4):
                        f = 4 * t + j
                        if last:
                            ins = dve.tensor_scalar(xw[:, f, :], xw[:, f, :], N_FIN[:, f:f + 1], None, ALU.mult)
                        else:
                            ins = dve.tensor_scalar(xw[:, f, :], xw[:, f, :], gm[:, k, f:f + 1],
                                                    mods[:, 48 * k + f:48 * k + f + 1], ALU.mult, ALU.add)
                    ins.then_inc(sem("h_ready"), 1)
                if last:
                    return
                for t in range(4):
                    dve.wait_ge(sem("h_hi"), 4 * k + t + 1)
                    dve.tensor_tensor(hs[:, 4 * t:4 * t + 4, 1, :], xw[:, 4 * t:4 * t + 4, :],
                                      hs[:, 4 * t:4 * t + 4, 0, :].bitcast(F32), ALU.subtract
                                      ).then_inc(sem("h_lo"), 1)

            def per_head(v, c=None):
                return v.unsqueeze(2).broadcast_to([P, HPG, HD])

            def ssd():
                for b in range(2):
                    dve.wait_ge(psum_free(b), r.q)
                dve.wait_ge(sem("wdt_hi"), 1)
                dve.tensor_tensor(wdtl[:, :, :], wdt[:, :, :], wdth[:, :, :].bitcast(F32), ALU.subtract
                                  ).then_inc(sem("wdt_lo"), 1)
                for half in range(2):
                    dve.tensor_copy(dcol[64 * half:64 * half + 64, :], hb[64 * half:64 * half + 64, 2, half:HEADS:2])
                dve.wait_ge(sem("a_exp"), 1)
                link(dve.tensor_scalar(hb[:, 3, :], hb[:, 3, :], -1.0, None, ALU.mult))
                dve.wait_ge(sem("dt_raw"), 1)
                link(dve.tensor_tensor(dtb[:, :, :], mps[:, 0, 0:64].rearrange("p (c h) -> p c h", c=2),
                                       hb[:, 1, :].unsqueeze(1).broadcast_to([P, 2, HEADS]), ALU.add))
                link(dve.tensor_scalar(dta[:, :, :], dtb[:, :, :], -1.0, None, ALU.mult))
                link(dve.tensor_tensor(dta[:, :, :], dta[:, :, :], dtb[:, :, :], ALU.max))
                link(dve.tensor_scalar(da[:, :, :], dtb[:, :, :], 0.0, None, ALU.max))
                dve.tensor_copy(css[:, 0, 0:1], ones[:, 0:1]).then_inc(sem("dt_abs"), 1)
                dve.wait_ge(sem("dt_exp"), 1)
                dve.tensor_scalar(dtb[:, :, :], dta[:, :, :], 1.0, None, ALU.add).then_inc(sem("dt_one_more"), 1)
                dve.wait_ge(sem("dt_one_more"), 1)
                link(dve.tensor_scalar(cs[:, :, :], dtb[:, :, :], -1.0, None, ALU.add))
                link(dve.tensor_tensor(cs[:, :, :], dta[:, :, :], cs[:, :, :], ALU.subtract))
                dve.wait_ge(sem("dt_ln"), 1)
                link(dve.reciprocal(wend[:, :, :], dtb[:, :, :]))
                link(dve.tensor_tensor(cs[:, :, :], cs[:, :, :], wend[:, :, :], ALU.mult))
                link(dve.tensor_tensor(dtv[:, :, :], dtv[:, :, :], cs[:, :, :], ALU.add))
                link(dve.tensor_tensor(dtv[:, :, :], dtv[:, :, :], da[:, :, :], ALU.add))
                dve.tensor_tensor(da[:, :, :], dtv[:, :, :], hb[:, 3, :].unsqueeze(1).broadcast_to([P, 2, HEADS]),
                                  ALU.mult).then_inc(sem("dt_a"), 1)
                dve.wait_ge(sem("dt_sums"), 1)
                two = [mps[:, w, 0:64].rearrange("p (c h) -> p c h", c=2) for w in (0, 1)]
                link(dve.tensor_copy(cs[:, :, :], two[0]))
                dve.tensor_tensor(wend[:, :, :], two[1], cs[:, :, :], ALU.subtract).then_inc(sem("wend_arg"), 1)
                dve.wait_ge(sem("decays"), 1)
                dve.tensor_copy(css[:, 0, 0:1], ones[:, 0:1]).then_inc(sem("ssd_group_done"), 1)

                with dve.Fori(0, GROUPS) as i:
                    one = i + 1
                    dve.wait_ge(sem("ssd_group_done"), one)
                    hsl = bass.ds(HPG * i, HPG)
                    dve.tensor_copy(das[:, :, :], da[:, :, hsl])
                    dve.tensor_copy(css[:, :, :], cs[:, :, hsl]).then_inc(sem("dt_staged"), 1)
                    dve.wait_ge(sem("x_tokens"), one)
                    for c in range(2):
                        ins = dve.tensor_tensor(xdt[:, c, :].rearrange("p (h d) -> p h d", h=HPG),
                                                mps[:, c, :].rearrange("p (h d) -> p h d", h=HPG),
                                                per_head(dtv[:, c, hsl]), ALU.mult)
                    ins.then_inc(sem("x_dt"), 1)
                    dve.wait_ge(sem("x_dt"), one)
                    dve.tensor_tensor(xde[:, :].rearrange("p (h d) -> p h d", h=HPG),
                                      xdt[:, 0, :].rearrange("p (h d) -> p h d", h=HPG),
                                      per_head(wend[:, 0, hsl]), ALU.mult).then_inc(sem("x_to_end"), 1)
                    dve.wait_ge(sem("b_tokens"), one)
                    dve.tensor_tensor(cbm[:, :, :], mps[:, 2, P:3 * P].rearrange("p (c l) -> p c l", c=2),
                                      tri[:, :].unsqueeze(1).broadcast_to([P, 2, P]), ALU.mult).then_inc(sem("cb_causal"), 1)

                    def seg(c):
                        dve.wait_ge(sem(f"seg{c}"), one)
                        for h in range(HPG):
                            ins = dve.tensor_scalar(E[c][:, h, :], mps[:, h // 4, P * (h % 4):P * (h % 4) + P],
                                                    css[:, c, h:h + 1], 0.0, ALU.subtract, ALU.min)
                        ins.then_inc(sem(f"seg_in{c}"), 1)

                    def decay(c):
                        dve.wait_ge(sem(f"seg_exp{c}"), one)
                        dve.wait_ge(sem("cb_causal"), one)
                        dve.tensor_tensor(E[c][:, :, :], E[c][:, :, :],
                                          cbm[:, c, :].unsqueeze(1).broadcast_to([P, HPG, P]), ALU.mult
                                          ).then_inc(sem(f"scores{c}"), 1)

                    seg(0)
                    decay(0)
                    dve.wait_ge(sem("y_off"), one)
                    dve.tensor_tensor(yof[:, :].rearrange("p (h d) -> p h d", h=HPG),
                                      mps[:, 3, :].rearrange("p (h d) -> p h d", h=HPG),
                                      per_head(ecs[:, 1, hsl]), ALU.mult).then_inc(sem("y_off_kept"), 1)
                    seg(1)
                    decay(1)
                    dve.wait_ge(sem("y_diag1"), one)
                    dve.wait_ge(sem("y_off_kept"), one)
                    dve.tensor_tensor(ytok[:, 1, :], mps[:, 3, :], yof[:, :], ALU.add).then_inc(sem("y_tok1"), 1)
                    dve.wait_ge(sem("y_features"), one)
                    y = E[1][:, :, :].rearrange("p a b -> p (a b)").rearrange("p (a b) -> p a b", a=4)
                    for j in range(4):
                        ins = dve.scalar_tensor_tensor(
                            out=y[:, j, :], in0=xst[:, j, :],
                            scalar=dcol[:, bass.ds(4 * i + j, 1)], in1=mps[:, j // 2, S * (j % 2):S * (j % 2) + S],
                            op0=ALU.mult, op1=ALU.add)
                    ins.then_inc(sem("y_skip"), 1)
                    dve.wait_ge(sem("y_skip"), one)
                    dve.tensor_tensor(y, y, zb[:, bass.ds(4 * i, 4), :], ALU.mult).then_inc(sem("y_gated"), 1)
                    dve.wait_ge(sem("y_sums"), one)
                    dve.tensor_scalar(var[:, :], mps[:, 2, 0:S], 1.0 / (HPG * HD), EPS, ALU.mult, ALU.add
                                      ).then_inc(sem("y_var"), 1)
                    dve.wait_ge(sem("y_dev"), one)
                    dve.reciprocal(rs[:, :], rs[:, :]).then_inc(sem("y_rs"), 1)
                    dve.wait_ge(sem("y_rs"), one)
                    for j in range(4):
                        yt = xbc[:, bass.ds(4 * i + j, 1), :].rearrange("p a s -> p (a s)")
                        ins = dve.scalar_tensor_tensor(out=yt, in0=y[:, j, :], scalar=N_SSD[:, bass.ds(4 * i + j, 1)],
                                                       in1=rs[:, :], op0=ALU.mult, op1=ALU.mult)
                    ins.then_inc(sem("ssd_group_done"), 1)

            def s5():
                dve.wait_ge(sem("ssd_group_done"), GROUPS + 1)
                v = [sp[:, j, :] for j in range(24)]
                (dt, ld, kk, th, la, tnh, sn, sh, cosv, em1, ang, nr, ai, den, kr, ki, lr, li, q, w, e0, e1,
                 _, spare) = v

                def tt(o, x, y, op):
                    link(dve.tensor_tensor(o, x, y, op))

                def tsc(o, x, s1, op1, s2=None, op2=None):
                    if op2 is None:
                        link(dve.tensor_scalar(o, x, s1, None, op1))
                    else:
                        link(dve.tensor_scalar(o, x, s1, s2, op1, op2))

                for half in range(2):
                    ins = dve.tensor_copy(ld[64 * half:64 * half + 64, :], ldt[64 * half:64 * half + 64, half:S5G:2])
                ins.then_inc(sem("s5_logdt"), 1)
                tsc(lr, LAM_RE, -1e-4, ALU.min)
                dve.wait_ge(sem("s5_dt"), 1)
                tt(la, lr, dt, ALU.mult)
                tt(ang, LAM_IM, dt, ALU.mult)
                tsc(kk, ang, 1.0 / TWO_PI, ALU.mult, ROUND, ALU.add)
                tsc(kk, kk, -ROUND, ALU.add)
                for part in (PI_A, PI_B, PI_C):
                    tsc(th, kk, -part, ALU.mult)
                    tt(ang, ang, th, ALU.add)
                link(dve.tensor_scalar(th, ang, PI_IN, -PI_IN, ALU.min, ALU.max))
                dve.tensor_copy(css[:, 0, 0:1], ones[:, 0:1]).then_inc(sem("s5_angle"), 1)
                dve.wait_ge(sem("s5_sines"), 1)
                tsc(q, tnh, -1.0, ALU.mult, 1.0, ALU.add)
                link(dve.reciprocal(q, q))
                tt(em1, tnh, q, ALU.mult)
                tsc(em1, em1, 2.0, ALU.mult)
                tt(w, sh, sh, ALU.mult)
                tsc(w, w, -2.0, ALU.mult)
                tsc(cosv, w, 1.0, ALU.add)
                tsc(mag[:, :], em1, 1.0, ALU.add)
                tt(nr, em1, cosv, ALU.mult)
                tt(nr, nr, w, ALU.add)
                tt(ai, mag[:, :], sn, ALU.mult)
                tsc(li, LAM_IM, 1.0, ALU.mult)
                tt(den, lr, lr, ALU.mult)
                tt(q, li, li, ALU.mult)
                tt(den, den, q, ALU.add)
                link(dve.reciprocal(den, den))
                tt(kr, nr, lr, ALU.mult)
                tt(q, ai, li, ALU.mult)
                tt(kr, kr, q, ALU.add)
                tt(kr, kr, den, ALU.mult)
                tt(ki, ai, lr, ALU.mult)
                tt(q, nr, li, ALU.mult)
                tt(ki, ki, q, ALU.subtract)
                tt(ki, ki, den, ALU.mult)
                dve.wait_ge(sem("s5_in"), 64)
                krb, kib = (t.unsqueeze(2).broadcast_to([P, ST, S5I]) for t in (kr, ki))
                tt(bbar[:, 0], krb, bnat[:, 0], ALU.mult)
                tt(q1[:, :, :], kib, bnat[:, 1], ALU.mult)
                tt(bbar[:, 0], bbar[:, 0], q1[:, :, :], ALU.subtract)
                tt(bbar[:, 1], krb, bnat[:, 1], ALU.mult)
                tt(q1[:, :, :], kib, bnat[:, 0], ALU.mult)
                tt(bbar[:, 1], bbar[:, 1], q1[:, :, :], ALU.add)
                tsc(e0, cosv, 1.0, ALU.mult)
                tsc(e1, sn, 1.0, ALU.mult)
                for which in (2, 0):
                    cw, sw = rot[:, which], rot[:, which + 1]
                    link(dve.memset(cw[:, :, 0:1], 1.0))
                    link(dve.memset(sw[:, :, 0:1], 0.0))
                    n = 1
                    while n < 16:
                        b0, b1 = (t.unsqueeze(2).broadcast_to([P, ST, n]) for t in (e0, e1))
                        tt(q1[:, :, 0:n], cw[:, :, 0:n], b0, ALU.mult)
                        tt(q2[:, :, 0:n], sw[:, :, 0:n], b1, ALU.mult)
                        tt(cw[:, :, n:2 * n], q1[:, :, 0:n], q2[:, :, 0:n], ALU.subtract)
                        tt(q1[:, :, 0:n], cw[:, :, 0:n], b1, ALU.mult)
                        tt(q2[:, :, 0:n], sw[:, :, 0:n], b0, ALU.mult)
                        tt(sw[:, :, n:2 * n], q1[:, :, 0:n], q2[:, :, 0:n], ALU.add)
                        tt(q, e0, e1, ALU.mult)
                        tt(w, e1, e1, ALU.mult)
                        tt(e0, e0, e0, ALU.mult)
                        tt(e0, e0, w, ALU.subtract)
                        tsc(e1, q, 2.0, ALU.mult)
                        n *= 2
                dve.tensor_copy(css[:, 0, 0:1], ones[:, 0:1]).then_inc(sem("s5_constants"), 1)
                with dve.Fori(0, UT) as i:
                    one = i + 1
                    dve.wait_ge(sem("s5_tile_done"), one)
                    for j in range(2):
                        dve.tensor_tensor(bblk[:, j], bbar[:, j, bass.ds(4 * i, 4), :].unsqueeze(2)
                                          .broadcast_to([P, 4, 8, S5I]),
                                          maskb[:, :, :].unsqueeze(3).broadcast_to([P, 4, 8, S5I]), ALU.mult)
                        ins = dve.tensor_tensor(cblk[:, j], cnat[:, j, bass.ds(i, 1), :].broadcast_to([P, 8, S5P]),
                                                maskc[:, j, :].unsqueeze(2).broadcast_to([P, 8, S5P]), ALU.mult)
                    ins.then_inc(sem("s5_blocks"), 1)
                    bu = [mps[:, 2 * j:2 * j + 2, :].rearrange("p a (b s) -> p (a b) s", b=2) for j in range(2)]
                    dve.wait_ge(sem("rot_ready"), one)
                    dve.wait_ge(sem("bu_ready"), one)
                    A = [t[:, :, :] for t in (tc, ts, t1, t2, wr, wi)]
                    C_, S_, T1, T2, WR, WI = A
                    dve.tensor_tensor(WR, C_, bu[0], ALU.mult)
                    dve.tensor_tensor(T1, S_, bu[1], ALU.mult)
                    dve.tensor_tensor(WI, C_, bu[1], ALU.mult)
                    dve.tensor_tensor(T2, S_, bu[0], ALU.mult).then_inc(sem("unrot_products"), 1)
                    dve.wait_ge(sem("unrot_products"), one)
                    dve.tensor_tensor(WR, WR, T1, ALU.add)
                    dve.tensor_tensor(WI, WI, T2, ALU.subtract).then_inc(sem("unrotated"), 1)
                    dve.wait_ge(sem("unrotated"), one)
                    for j in range(4):
                        m = mag[:, bass.ds(4 * i + j, 1)].broadcast_to([P, S])
                        dve.tensor_tensor_scan(t1[:, j, :], m, wr[:, j, :], 0.0, ALU.mult, ALU.add)
                        ins = dve.tensor_tensor_scan(t2[:, j, :], m, wi[:, j, :], 0.0, ALU.mult, ALU.add)
                    ins.then_inc(sem("scanned"), 1)
                    dve.wait_ge(sem("scanned"), one)
                    dve.tensor_tensor(WR, C_, T1, ALU.mult)
                    dve.tensor_tensor(WI, S_, T2, ALU.mult).then_inc(sem("rot_half"), 1)
                    dve.wait_ge(sem("rot_half"), one)
                    dve.tensor_tensor(WR, WR, WI, ALU.subtract).then_inc(sem("s_re"), 1)
                    dve.tensor_tensor(S_, S_, T1, ALU.mult)
                    dve.tensor_tensor(C_, C_, T2, ALU.mult).then_inc(sem("rot_rest"), 1)
                    dve.wait_ge(sem("rot_rest"), one)
                    dve.wait_ge(sem("s_re"), one)
                    dve.tensor_tensor(WI, S_, C_, ALU.add).then_inc(sem("s_im"), 1)
                    dve.wait_ge(sem("s5_out"), one)
                    dve.scalar_tensor_tensor(out=sil[:, 1, :], in0=sil[:, 0, :], scalar=S5_D[:, bass.ds(i, 1)],
                                             in1=mps[:, 0, 0:S], op0=ALU.mult, op1=ALU.add).then_inc(sem("s5_y"), 1)
                    dve.wait_ge(sem("s5_gelu"), one)
                    dve.tensor_copy(ub[:, bass.ds(i, 1), :].rearrange("p a s -> p (a s)"), var[:, :]
                                    ).then_inc(sem("s5_tile_done"), 1)

            def split():
                dve.wait_ge(sem("y_hi"), 1)
                dve.tensor_tensor(hs[:, :, 1, :], xbc[:, 0:NT, :], hs[:, :, 0, :].bitcast(F32), ALU.subtract
                                  ).then_inc(sem("y_lo"), 1)
                dve.wait_ge(sem("y_hi"), 2)
                dve.tensor_tensor(ybs[:, :, 1, :], ub[:, :, :], ybs[:, :, 0, :].bitcast(F32), ALU.subtract
                                  ).then_inc(sem("y_lo"), 1)

            todo = list(weights)
            for kind, ph in steps:
                if kind == "norm":
                    norm(ph)
                    if ph == 0:
                        first_two(todo[0])
                elif kind == "gemm":
                    todo.pop(0)
                    if ph.evac == "resid" and ph.row == 0:
                        dve.wait_ge(sem("ada_done"), r.c)
                        gates(ph.gate)
                    gemm(ph, todo[0] if todo else None)
                elif kind == "ssd":
                    ssd()
                elif kind == "s5":
                    s5()
                elif kind == "split":
                    split()
                elif kind == "final":
                    norm(3, last=True)

        @block.tensor
        def _(pe):
            r = Run()

            def ada_end(c):
                pe.wait_ge(sem("ada_quarter"), c * 4 + 4)
                for j in range(4):
                    ins = mm(pe, mps[:, 3, j:j + 1], acc[:, P * j:P * j + P], ones[:, 0:1], True, True)
                ins.then_inc(sem("ada_sum"), 1)

            pe.wait_ge(sem("masks"), 1)
            pe.wait_ge(sem("rows_in"), 14 * 16)
            for j in range(4):
                ins = pe.transpose(mps[:, 0, P * j:P * j + P], rows[:, j, :], ident[:, :])
            ins.then_inc(sem("rows_turned"), 1)
            pe.wait_ge(sem("x_in"), 16)
            for t in range(4):
                if t >= 2:
                    pe.wait_ge(sem("x_ready"), t - 1)
                for j in range(4):
                    for c in range(2):
                        f = 4 * t + j
                        ins = pe.transpose(gps[:, t % 2, j, P * c:P * c + P], xin[:, c, P * f:P * f + P], ident[:, :])
                ins.then_inc(sem("x_turned"), 1)
            pe.wait_ge(sem("x_ready"), 4)
            pe.wait_ge(sem("vectors"), 1)
            with pe.Fori(0, 8) as i:
                if True:
                    ada_end(i)
            r.c = 8

            def gemm(ph, n0, m0):
                per, mper = len(ph.stream), 2 * ph.slabs
                moving = {"h": hs, "ff": ffs, "yb": ybs}[ph.moving]
                if ph.moving == "ff":
                    pe.wait_ge(sem("prod_free"), r.p + 1)
                elif ph.name == "w_out":
                    pe.wait_ge(sem("prod_free"), r.p + 1)
                elif ph.name == "a_proj":
                    pe.wait_ge(sem("y_lo"), 1)
                elif ph.name == "b_glu":
                    pe.wait_ge(sem("y_lo"), 2)

                def body(i):
                    for g in range(2):
                        if isinstance(i, int) and r.q + i == 0:
                            pass
                        else:
                            pe.wait_ge(psum_free(g), r.q + i)
                        tiles = [0, 2] if ph.narrow and g == 1 else [0, 1, 2, 3]
                        for pos, (what, gg, s) in enumerate(ph.stream):
                            if what != "w" or gg != g:
                                continue
                            mp = g * ph.slabs + s
                            pe.wait_ge(raw_used, n0 + i * per + pos + 1)
                            k0 = sum(ph.chunks[:s])
                            for j in tiles:
                                for k in range(ph.chunks[s]):
                                    hi = whi[:, mp % SPLIT, k, P * j:P * j + P]
                                    lo = wlo[:, mp % SPLIT, k, P * j:P * j + P]
                                    xh, xl = moving[:, k0 + k, 0, :], moving[:, k0 + k, 1, :]
                                    out = gps[:, g, j, :]
                                    mm(pe, out, hi, xh, k0 + k == 0 and j % 2 == 0, False)
                                    mm(pe, out, hi, xl, False, False)
                                    ins = mm(pe, out, lo, xh, False, k0 + k == sum(ph.chunks) - 1)
                            ins.then_inc(slab_done, 1)
                    if ph.ada:
                        ada_end(r.c + i)

                start = 0
                if r.q == 0:
                    body(0)
                    start = 1
                if ph.bodies - start > 1:
                    with pe.Fori(start, ph.bodies) as i:
                        body(i)
                elif ph.bodies - start == 1:
                    body(start)
                r.q += ph.bodies
                r.c += ph.ada * ph.bodies
                if ph.evac in ("pair", "glu"):
                    r.p += 2 * ph.bodies

            def norm(k):
                for t in range(4):
                    pe.wait_ge(sem("squares"), 4 * k + t + 1)
                    for j in range(4):
                        f = 4 * t + j
                        ins = mm(pe, mps[:, 2, 0:S], ones[:, :], xw[:, f, :], f == 0, f == NT - 1)
                ins.then_inc(sem("sum_squares"), 1)

            def ssd():
                for b in range(2):
                    pe.wait_ge(psum_free(b), r.q)
                pe.wait_ge(sem("ada_done"), r.c)
                pe.wait_ge(sem("wdt_lo"), 1)
                for c in range(2):
                    tok = slice(P * c, P * c + P)
                    out = mps[:, 0, HEADS * c:HEADS * c + HEADS]
                    for k in range(NT):
                        mm(pe, out, hs[:, k, 0, tok], wdth[:, k, :], k == 0 and c == 0, False)
                        mm(pe, out, hs[:, k, 1, tok], wdth[:, k, :], False, False)
                        ins = mm(pe, out, hs[:, k, 0, tok], wdtl[:, k, :], False, k == NT - 1)
                ins.then_inc(sem("dt_raw"), 1)
                pe.wait_ge(sem("dt_a"), 1)
                dav = da[:, :, :].rearrange("p c h -> p (c h)")
                mm(pe, mps[:, 0, 0:64], tri[:, :], dav, True, True)
                mm(pe, mps[:, 1, 0:64], ones[:, :], dav, True, True).then_inc(sem("dt_sums"), 1)
                with pe.Fori(0, GROUPS) as i:
                    one = i + 1
                    pe.wait_ge(sem("ssd_group_done"), one)
                    pe.wait_ge(sem("ssd_staged"), one)
                    for c in range(2):
                        for j in range(4):
                            ins = pe.transpose(mps[:, c, P * j:P * j + P], xst[:, j, P * c:P * c + P], ident[:, :])
                    ins.then_inc(sem("x_tokens"), 1)
                    pe.transpose(mps[:, 2, 0:P], bst[:, 0:P], ident[:, :])
                    for c in range(2):
                        tok = slice(P * c, P * c + P)
                        ins = mm(pe, mps[:, 2, P * (c + 1):P * (c + 2)], bst[:, tok], cst[:, tok], c == 0, c == 1)
                    ins.then_inc(sem("b_and_cb"), 1)

                    def seg(c):
                        for h in range(HPG):
                            ins = mm(pe, mps[:, h // 4, P * (h % 4):P * (h % 4) + P],
                                     das[:, c, h:h + 1].broadcast_to([P, P]), tri[:, :], h % 4 == 0, h % 4 == 3)
                        ins.then_inc(sem(f"seg{c}"), 1)

                    def diag(c):
                        pe.wait_ge(sem(f"scores{c}"), one)
                        for h in range(HPG):
                            ins = mm(pe, mps[:, 2 + c, HD * h:HD * h + HD], E[c][:, h, :], xdt[:, c, HD * h:HD * h + HD],
                                     h == 0, h == HPG - 1)
                        ins.then_inc(sem(f"y_diag{c}"), 1)

                    pe.wait_ge(sem("dt_staged"), one)
                    pe.wait_ge(sem("x_dt"), one)
                    seg(0)
                    pe.wait_ge(sem("x_to_end"), one)
                    pe.wait_ge(sem("b_tokens"), one)
                    mm(pe, mps[:, 3, :], btok[:, :], xde[:, :], True, True).then_inc(sem("state"), 1)
                    pe.wait_ge(sem("state_kept"), one)
                    mm(pe, mps[:, 3, :], cst[:, P:2 * P], prev[:, :], True, True).then_inc(sem("y_off"), 1)
                    pe.wait_ge(sem("seg_in0"), one)
                    seg(1)
                    diag(0)
                    pe.wait_ge(sem("y_off_kept"), one)
                    diag(1)
                    pe.wait_ge(sem("y_tok0"), one)
                    pe.wait_ge(sem("y_tok1"), one)
                    for j in range(4):
                        for c in range(2):
                            at_ = S * (j % 2) + P * c
                            ins = pe.transpose(mps[:, j // 2, at_:at_ + P], ytok[:, c, P * j:P * j + P], ident[:, :])
                    ins.then_inc(sem("y_features"), 1)
                    pe.wait_ge(sem("y_squares"), one)
                    sq = E[0][:, :, :].rearrange("p a b -> p (a b)")
                    for j in range(4):
                        ins = mm(pe, mps[:, 2, 0:S], ones[:, :], sq[:, S * j:S * j + S], j == 0, j == 3)
                    ins.then_inc(sem("y_sums"), 1)

            def s5():
                pe.wait_ge(sem("ssd_group_done"), GROUPS + 1)
                with pe.Fori(0, UT) as i:
                    one = i + 1
                    pe.wait_ge(sem("s5_tile_done"), one)
                    pe.wait_ge(sem("s5_blocks"), one)
                    bf = bblk[:, :, :, :, :].rearrange("p r j g i -> p (r j) (g i)")
                    cf = cblk[:, :, :, :].rearrange("p r g s -> p (r g s)")
                    for t in range(8):
                        pe.transpose(mps[:, t // 4, P * (t % 4):P * (t % 4) + P], bf[:, t, :], ident[:, :])
                        ins = pe.transpose(mps[:, 2 + t // 4, P * (t % 4):P * (t % 4) + P], cf[:, P * t:P * t + P],
                                           ident[:, :])
                    ins.then_inc(sem("s5_turned"), 1)
                    pe.wait_ge(sem("u_staged"), one)
                    pe.wait_ge(sem("s5_mats"), one)
                    for rim in range(2):
                        for j in range(4):
                            ins = mm(pe, mps[:, 2 * rim + j // 2, S * (j % 2):S * (j % 2) + S], btb[:, rim, j, :],
                                     sil[:, 0, :], j % 2 == 0, j % 2 == 1)
                    ins.then_inc(sem("bu_ready"), 1)
                    for rim, states in enumerate((wr, wi)):
                        pe.wait_ge(sem("s_re" if rim == 0 else "s_im"), one)
                        for j in range(4):
                            ins = mm(pe, mps[:, 0, 0:S], ctb[:, rim, j, :], states[:, j, :], rim + j == 0,
                                     rim == 1 and j == 3)
                    ins.then_inc(sem("s5_out"), 1)

            def final():
                norm(3)
                for t in range(4):
                    pe.wait_ge(sem("h_ready"), 12 + t + 1)
                    for c in range(2):
                        if t or c:
                            if t:
                                pe.wait_ge(sem("y_out"), 2 * (t - 1) + c + 1)
                        for j in range(4):
                            ins = pe.transpose(mps[:, c, P * j:P * j + P], xw[:, 4 * t + j, P * c:P * c + P], ident[:, :])
                        ins.then_inc(sem("y_turned"), 1)

            n, m = 32, 0
            for kind, ph in steps:
                if kind == "norm":
                    norm(ph)
                    pe.wait_ge(sem("h_lo"), 4 * ph + 4)
                elif kind == "gemm":
                    gemm(ph, n, m)
                    n += len(ph.stream) * ph.bodies
                    m += 2 * ph.slabs * ph.bodies
                elif kind == "ssd":
                    ssd()
                elif kind == "s5":
                    s5()
                elif kind == "final":
                    final()


_INS = ["x", "c", "w_ada", "b_ada", "norm_ffn1", "w_ffn1_in", "w_ffn1_out", "norm_mix", "w_in", "conv_w", "conv_b",
        "dt_bias", "a_log", "d_ssd", "ssd_norm_w", "w_a_proj", "s5_lambda_re", "s5_lambda_im", "s5_b_re", "s5_b_im",
        "s5_c_re", "s5_c_im", "s5_d", "s5_log_dt", "w_b_glu", "w_out", "norm_ffn2", "w_ffn2_in", "w_ffn2_out",
        "norm_final"]


def kernel(**inputs):
    import numpy as np
    import concourse.bacc as bacc
    from concourse.bass_utils import run_bass_kernel_spmd

    nc = bacc.Bacc("TRN2", target_bir_lowering=False, num_devices=1)
    arrays, aps = {}, {}
    for name in _INS:
        v = np.ascontiguousarray(inputs[name])
        arrays[f"in_{name}_dram"] = v
        aps[name] = nc.dram_tensor(f"in_{name}_dram", v.shape, mybir.dt.from_np(v.dtype), kind="ExternalInput").ap()
    aps["out"] = nc.dram_tensor("out_dram", (1, S, D), F32, kind="ExternalOutput").ap()
    build(nc, aps)
    r = run_bass_kernel_spmd(nc, [arrays], core_ids=[0])
    return r.results[0]["out_dram"]
```

```python
from contextlib import ExitStack

import concourse.bass as bass
from concourse import mybir

F32 = mybir.dt.float32
F32R = mybir.dt.float32r
ACT = mybir.ActivationFunctionType
ALU = mybir.AluOpType

P = 128
D = 2048
S = 256
FF = 5504
NT = D // P
FT = FF // P
HEADS, HD, GROUPS, NST = 32, 64, 4, 128
HPG = HEADS // GROUPS
CONVD = D + 2 * GROUPS * NST
CT = CONVD // P
KW = 4
OFF_XBC = D
OFF_DT = OFF_XBC + CONVD
OFF_U = OFF_DT + HEADS
U = 1024
UT = U // P
S5G, S5I, S5P = 64, 16, 64
ST = S5G * S5P // P
OFF_GATES = OFF_U + U
EPS = 1e-6
COLS = 512
RING = 4
SPLIT = 2
FF1 = 20
TWO_PI = 6.283185307179586
PI_A, PI_B = 6.28125, 0.0019350051879882812
PI_C = TWO_PI - PI_A - PI_B
ROUND = 1.5 * 2.0 ** 23
PI_IN = 3.1415925


class Phase:

    def __init__(self, name, weight, col, k_tiles, bodies, evac, moving, ada=False, pair=0, row=0,
                 narrow=False, start=0, gate=None, last=False, side=False, q0=0):
        self.name, self.weight, self.col, self.bodies, self.evac = name, weight, col, bodies, evac
        self.moving, self.ada, self.pair, self.row, self.narrow = moving, ada, pair, row, narrow
        self.start, self.gate, self.last, self.side, self.q0 = start, gate, last, side, q0
        n = 6 if k_tiles > 16 else (k_tiles + 3) // 4
        self.chunks = [4] * n
        if k_tiles == 20:
            self.chunks = [4, 4, 3, 3, 3, 3]
        elif k_tiles == 23:
            self.chunks = [4, 4, 4, 4, 4, 3]
        assert sum(self.chunks) == k_tiles
        self.slabs = n
        self.stream = [("w", 0, s) for s in range(n)]
        for s in range(n):
            self.stream.append(("w", 1, s))
            if ada:
                self.stream += [("ada", 0, t) for t in range(4) if t * min(n, 4) // 4 == s]
        at = [k for k, (what, _, _) in enumerate(self.stream) if what == "ada"]
        self.back = [0] + [at[t] - at[t - 1] for t in range(1, 4)] if ada else []
        assert len(self.stream) % RING == 0 and n % SPLIT == 0


def plan():
    def ffn(n, gate):
        win, wout = f"w_ffn{n}_in", f"w_ffn{n}_out"
        ada = n == 1
        first = [Phase("in", win, 0, NT, FF1 // 4, "pair", "h", True, pair=FF)] if ada else [
            Phase("in", win, 0, NT, 4, "pair", "h", True, pair=FF),
            Phase("in", win, 4 * COLS, NT, FF1 // 4 - 4, "pair", "h", False, pair=FF, start=8)]
        steps = [("gemm", p) for p in first]
        steps += [("s5_sines", None)] * ada
        steps += [("gemm", Phase("out", wout, 0, FF1, 2, "resid", "ff", ada, gate=gate))]
        steps += [("s5_reciprocals", None)] * ada
        steps += [("gemm", p) for p in (
            Phase("in", win, FF1 * P, NT, (FT - FF1) // 4, "pair", "h", ada, pair=FF),
            Phase("in", win, (FT - 3) * P, NT, 1, "pair", "h", ada, pair=FF, start=(FT - 3 - FF1) // 2, narrow=True),
            Phase("out", wout, 0, FT - FF1, 2, "resid", "ff", ada, gate=gate, row=FF1 * P, last=(n == 2)))]
        return steps

    return (
        [("prologue", None), ("norm", 0), ("s5_step", None)] + ffn(1, 0) + [("norm", 1)]
        + [("gemm", Phase("u", "w_in", OFF_U, NT, 1, "copy", "h", True)),
           ("dt", None), ("s5_begin", None),
           ("gemm", Phase("xbc", "w_in", OFF_XBC, NT, 3, "conv", "h", False, side="s5")),
           ("gemm", Phase("z", "w_in", 0, NT, 2, "silu", "h", False, side="s5")),
           ("s5_end", None),
           ("gemm", Phase("gate_a", "w_in", OFF_GATES, NT, 2, "sig_a", "h", True, side="ssd")),
           ("gemm", Phase("gate_b", "w_in", OFF_GATES + D, NT, 2, "sig_b", "h", True, side="ssd", last=True)),
           ("split", None),
           ("gemm", Phase("a_proj", "w_a_proj", 0, NT, 2, "mul_a", "h", True)),
           ("gemm", Phase("b_glu", "w_b_glu", 0, U // P, 4, "glu", "yb", False, pair=D)),
           ("gemm", Phase("w_out", "w_out", 0, NT, 2, "resid", "h", True, gate=1)),
           ("norm", 2)] + ffn(2, 2) + [("final", None)]
    )


class Run:

    def __init__(self):
        self.n = self.m = self.q = self.c = self.p = self.g = 0


def build(nc, a):
    steps = plan()
    with ExitStack() as ctx:
        small_base = [0]
        arena = ctx.enter_context(nc.sbuf_tensor("arena", [P, 53120], F32))
        base = nc.sbuf_base - 53120 * 4

        def at(name, offset, shape, dt=F32):
            size = 4
            for s in shape[1:]:
                size *= s
            assert offset + size <= 53120 * 4, (name, offset + size)
            return nc.alloc_sbuf_tensor_at(name, shape, dt, offset=base + offset)

        def small(name, shape, dt=F32):
            size = 4
            for s in shape[1:]:
                size *= s
            size = (size + 31) // 32 * 32
            t = at(name, 200 * K + small_base[0], shape, dt)
            small_base[0] += size
            return t

        K = 1024
        xT = at("xT", 0, [P, NT, S])
        hs = at("hs", 16 * K, [P, NT, 2, S], F32R)
        raw = at("raw", 48 * K, [P, RING, 4, COLS])
        whi = at("whi", 80 * K, [P, SPLIT, 4, COLS], F32R)
        wlo = at("wlo", 96 * K, [P, SPLIT, 4, COLS], F32R)
        R = 112 * K
        W = R + 48 * K
        ffs = at("ffs", R, [P, FT - FF1, 2, S], F32R)
        xw = at("xw", R + 48 * K, [P, NT, S])
        xbc = at("xbc", R, [P, CT, S])
        ub = at("ub", R + 24 * K, [P, UT, S])
        zb = at("zb", R + 32 * K, [P, NT, S])
        ga = at("ga", 0, [P, NT, S])
        gb = at("gb", R + 32 * K, [P, NT, S])
        ybs = at("ybs", R + 64 * K, [P, UT, 2, S], F32R)
        wdt = at("wdt", W + 8 * K, [P, NT, HEADS])
        wdth = at("wdth", W + 10 * K, [P, NT, HEADS], F32R)
        wdtl = at("wdtl", W + 12 * K, [P, NT, HEADS], F32R)
        xdt = at("xdt", W + 6 * K, [P, 2, HPG * HD])
        xde = at("xde", W + 10 * K, [P, HPG * HD])
        prev = at("prev", W + 12 * K, [P, HPG * HD])
        yof = at("yof", W + 14 * K, [P, HPG * HD])
        E = [at(f"E{c}", W + (16 + 4 * c) * K, [P, HPG, P]) for c in range(2)]
        ytok = at("ytok", W + 24 * K, [P, 2, HPG * HD])
        cbm = at("cbm", W + 28 * K, [P, 2, P])
        btok = at("btok", W + 29 * K, [P, P])
        t1 = at("t1", 0, [P, 4, S])
        t2 = at("t2", 4 * K, [P, 4, S])
        wr = at("wr", 8 * K, [P, 4, S])
        wi = at("wi", 12 * K, [P, 4, S])
        tc = at("tc", W, [P, 4, S])
        ts = at("ts", W + 4 * K, [P, 4, S])
        ctb = at("ctb", W + 8 * K, [P, 2, 4, P])
        btb = at("btb", W + 12 * K, [P, 2, 4, P])
        bblk = at("bblk", R + 40 * K, [P, 2, 4, 8, S5I])
        cblk = at("cblk", R + 44 * K, [P, 2, 8, S5P])
        rscr = at("rscr", R + 80 * K, [P, 4, S])
        Z = R + 64 * K
        bbar = at("bbar", Z, [P, 2, ST, S5I])
        cnat = at("cnat", Z + 4 * K, [P, 2, UT, S5P])
        rot = at("rot", Z + 8 * K, [P, 4, ST, 16])
        bnat = at("bnat", W, [P, 2, ST, S5I])
        q1 = at("q1", W + 4 * K, [P, ST, S5I])
        q2 = at("q2", W + 6 * K, [P, ST, S5I])
        sp = at("sp", W + 8 * K, [P, 24, ST])
        T = R + 80 * K
        sil = at("sil", T, [P, 2, S])
        prod = at("prod", T + 2 * K, [P, 2, S])
        acc = at("acc", T + 4 * K, [P, COLS])
        var = at("var", T + 6 * K, [P, S])
        rs = at("rs", T + 7 * K, [P, S])
        xin = at("xin", R, [P, 2, D])
        rows = at("rows", R + 16 * K, [P, 4, P])
        ones_i = at("ones_i", R + 18 * K, [P, P])
        xout = at("xout", R, [P, 2, D])

        mods = small("mods", [P, 9 * NT])
        gm = small("gm", [P, 3, NT])
        hg = small("hg", [P, 3, NT])
        pv = small("pv", [P, 4, P])
        ident = small("ident", [P, P])
        ones = small("ones", [P, P])
        tri = small("tri", [P, P])
        cact = small("cact", [P, NT])
        maskb = small("maskb", [P, 4, 8])
        maskc = small("maskc", [P, 2, 8])
        dcol = small("dcol", [P, NT])
        mag = small("mag", [P, ST])
        hb = small("hb", [P, 4, HEADS])
        ldt = small("ldt", [P, S5G])
        dtv = small("dtv", [P, 2, HEADS])
        da = small("da", [P, 2, HEADS])
        cs = small("cs", [P, 2, HEADS])
        wend = small("wend", [P, 2, HEADS])
        ecs = small("ecs", [P, 2, HEADS])
        dta = small("dta", [P, 2, HEADS])
        dtb = small("dtb", [P, 2, HEADS])
        tick = small("tick", [P, 8])
        assert small_base[0] <= 53120 * 4 - 200 * K

        x_kept = nc.dram_tensor("x_kept", (P, NT * S), F32, kind="Internal").ap()

        gps = ctx.enter_context(nc.psum_tensor("gps", [P, 2, 4, S], F32))
        mps = ctx.enter_context(nc.psum_tensor("mps", [P, 4, 512], F32))

        C_IN, N_FFN1, N_MIX, N_FFN2, N_FIN, N_SSD, CONV_B, S5_D = (pv[:, 0, i:i + w] for i, w in (
            (0, 16), (16, 16), (32, 16), (48, 16), (64, 16), (80, 16), (96, 24), (120, 8)))
        CONV_W = pv[:, 1, 0:96]
        LAM_RE = pv[:, 1, 96:128]
        B_ADA = pv[:, 2:4, :].rearrange("p a b -> p (a b)")[:, 0:9 * NT]
        LAM_IM = pv[:, 3, 16:48]
        NORMS = [N_FFN1, N_MIX, N_FFN2]

        sems = {}

        def sem(name):
            if name not in sems:
                sems[name] = ctx.enter_context(nc.semaphore(name))
            return sems[name]

        def landed(slot):
            return sem(f"slab_landed{slot}")

        def psum_free(b):
            return sem(f"outputs_read{b}")

        raw_used, hi_ready, slab_done = sem("slab_used"), sem("hi_ready"), sem("slab_multiplied")
        block = ctx.enter_context(nc.Block())

        def mm(pe, out, lhsT, rhs, start, stop):
            return pe.matmul(out, lhsT, rhs, start=start, stop=stop, skip_group_check=True)

        @block.sync
        def _(sync):
            r = Run()
            x_t = a["x"][0].rearrange("(c p) d -> p c d", p=P)
            sync.dma_start(xin[:, :, :], x_t).then_inc(sem("x_in"), 16)

            vec_list = [("c", a["c"][0], 0, 0), ("n1", a["norm_ffn1"][0], 16, 0), ("nm", a["norm_mix"][0], 32, 0),
                        ("n2", a["norm_ffn2"][0], 48, 0), ("nf", a["norm_final"], 64, 0),
                        ("sn", a["ssd_norm_w"][0], 80, 0), ("cb", a["conv_b"][0], 96, 0),
                        ("sd", a["s5_d"][0].rearrange("g i -> (g i)"), 120, 0),
                        ("cw", a["conv_w"][0].rearrange("k c -> (k c)"), 0, 1),
                        ("lr", a["s5_lambda_re"][0].rearrange("g p -> (g p)"), 96, 1),
                        ("b1", a["b_ada"][0][0:P * P], 0, 2), ("b2", a["b_ada"][0][P * P:], 0, 3),
                        ("li", a["s5_lambda_im"][0].rearrange("g p -> (g p)"), 16, 3),
                        ("pad", a["b_ada"][0][0:80 * P], 48, 3)]
            for _, v, row, tile in vec_list:
                v = v.rearrange("(t p) -> t p", p=P)
                sync.dma_start(rows[row:row + v.shape[0], tile, :], v).then_inc(sem("rows_in"), 16)
            for j, name in enumerate(("a_log", "dt_bias", "d_ssd")):
                sync.dma_start(hb[:, j, :], a[name][0:1, :].broadcast_to([P, HEADS])).then_inc(sem("heads_in"), 16)
            sync.dma_start(ldt[:, :], a["s5_log_dt"][0:1, :].broadcast_to([P, S5G])).then_inc(sem("heads_in"), 16)

            def slab(n, pos, src_parts, by_tensor=None):
                if by_tensor is not None:
                    sync.wait_ge(sem("ada_products"), by_tensor)
                elif not (isinstance(n, int) and n < RING):
                    sync.wait_ge(raw_used, n - (RING - 1))
                for dst, src in src_parts:
                    sync.dma_start(dst, src).then_inc(landed(pos % RING), 32 // len(src_parts))

            ada = a["w_ada"][0].rearrange("(k p) n -> p k n", p=P)

            def ada_slab(n, pos, c, s, by_tensor=None):
                slab(n, pos, [(raw[:, pos % RING, :, :], ada[:, 4 * s:4 * s + 4, bass.ds(c * COLS, COLS)])], by_tensor)

            for kind, ph in steps:
                if kind == "prologue":
                    for s in range(4):
                        ada_slab(s, s, 0, s)
                    with sync.Fori(1, 8) as i:
                        for s in range(4):
                            ada_slab(i * 4 + s, s, i, s, i if s == 0 else None)
                    sync.wait_ge(sem("ada_products"), 8)
                    r.n, r.c = 32, 8
                elif kind == "gemm":
                    w = a[ph.weight][0][ph.row:ph.row + sum(ph.chunks) * P, :].rearrange("(k p) n -> p k n", p=P)
                    per = len(ph.stream)

                    def body(i, narrow=False):
                        for pos, (what, g, s) in enumerate(ph.stream):
                            n = r.n + i * per + pos
                            if what == "ada":
                                ada_slab(n, pos, r.c + i, s)
                                continue
                            k0, kc = sum(ph.chunks[:s]), ph.chunks[s]
                            dst = raw[:, pos % RING, 0:kc, :]
                            if ph.pair:
                                width = P if (ph.narrow and g == 1) else COLS // 2
                                col = ph.col + (i * 2 + g) * (COLS // 2)
                                parts = [(dst[:, :, h * COLS // 2:h * COLS // 2 + width],
                                          w[:, k0:k0 + kc, bass.ds(col + h * ph.pair, width)]) for h in range(2)]
                            else:
                                parts = [(dst, w[:, k0:k0 + kc, bass.ds(ph.col + (i * 2 + g) * COLS, COLS)])]
                            slab(n, pos, parts)

                    if ph.bodies > 1:
                        with sync.Fori(0, ph.bodies) as i:
                            body(i)
                    else:
                        body(0)
                    r.n += per * ph.bodies
                    r.c += ph.ada * ph.bodies
                elif kind == "final":
                    sync.wait_ge(sem("out_ready"), 1)
                    sync.dma_start(a["out"][0].rearrange("(c p) d -> p c d", p=P), xout[:, :, :]
                                   ).then_inc(sem("out_written"), 16)
                    sync.wait_ge(sem("out_written"), 16)

        @block.gpsimd
        def _(pool):
            def mask(t, pattern, base, mult, op, fill):
                pool.affine_select(out=t, in_=t, compare_op=op, fill=fill, base=base, pattern=pattern,
                                   channel_multiplier=mult).then_inc(sem("mask_step"), 1)

            pool.memset(ident[:, :], 0.0).then_inc(sem("mask_step"), 1)
            pool.memset(ones[:, :], 1.0).then_inc(sem("mask_step"), 1)
            pool.memset(tri[:, :], 1.0).then_inc(sem("mask_step"), 1)
            pool.memset(maskb[:, :, :], 0.0).then_inc(sem("mask_step"), 1)
            pool.memset(maskc[:, :, :], 1.0).then_inc(sem("mask_step"), 1)
            pool.wait_ge(sem("mask_step"), 5)
            mask(ident[:, :], [[-1, P]], 0, 1, ALU.not_equal, 1.0)
            mask(tri[:, :], [[1, P]], 0, -1, ALU.is_ge, 0.0)
            mask(maskc[:, 0, :], [[-16, 8]], 0, 1, ALU.is_ge, 0.0)
            pool.wait_ge(sem("mask_step"), 8)
            mask(maskc[:, 0, :], [[16, 8]], 15, -1, ALU.is_ge, 0.0)
            pool.wait_ge(sem("mask_step"), 9)
            for half in range(2):
                pool.memset(maskc[64 * half:64 * half + 64, 1, :], 0.0).then_inc(sem("mask_step"), 1)
            for j in range(4):
                for half in range(2):
                    g = 2 * j + half
                    pool.memset(maskb[64 * half:64 * half + 64, j, g:g + 1], 1.0).then_inc(sem("mask_step"), 1)
            pool.wait_ge(sem("mask_step"), 19)
            pool.tensor_scalar(maskc[:, 1, :], maskc[:, 0, :], -1.0, None, ALU.mult).then_inc(sem("masks"), 1)

            def link(ins):
                ins.then_inc(sem("pool_step"), 1)
                chain[0] += 1
                pool.wait_ge(sem("pool_step"), chain[0])

            chain = [0]

            def tt(o, x, y, op):
                link(pool.tensor_tensor(o, x, y, op))

            def tsc(o, x, s1, op1, s2=None, op2=None):
                if op2 is None:
                    link(pool.tensor_scalar(o, x, s1, None, op1))
                else:
                    link(pool.tensor_scalar(o, x, s1, s2, op1, op2))

            pool.wait_ge(sem("h_lo"), 4)
            for j, name in enumerate(("s5_b_re", "s5_b_im")):
                pool.dma_start(bnat[:, j, :, :], a[name][0].rearrange("(t g) p i -> (g p) t i", g=2)
                               ).then_inc(sem("s5_in"), 16)
            for j, name in enumerate(("s5_c_re", "s5_c_im")):
                pool.dma_start(cnat[:, j, :, :], a[name][0].rearrange("(t g) i p -> (g i) t p", g=8)
                               ).then_inc(sem("s5_in"), 16)
            v = [sp[:, j, :] for j in range(24)]
            (dt, ld, kk, th, la, tnh, sn, sh, cosv, em1, ang, nr, ai, den, kr, ki, lr, li, q, w, e0, e1,
             tq, spare) = v
            pool.wait_ge(sem("heads_in"), 64)
            for half in range(2):
                ins = pool.tensor_copy(ld[64 * half:64 * half + 64, :], ldt[64 * half:64 * half + 64, half:S5G:2])
            ins.then_inc(sem("s5_logdt"), 1)
            pool.wait_ge(sem("s5_logdt"), 1)
            pool.wait_ge(sem("vectors"), 1)
            tsc(lr, LAM_RE, -1e-4, ALU.min)
            pool.wait_ge(sem("s5_dt"), 1)
            tt(la, lr, dt, ALU.mult)
            tt(ang, LAM_IM, dt, ALU.mult)
            tsc(kk, ang, 1.0 / TWO_PI, ALU.mult, ROUND, ALU.add)
            tsc(kk, kk, -ROUND, ALU.add)
            for part in (PI_A, PI_B, PI_C):
                tsc(th, kk, -part, ALU.mult)
                tt(ang, ang, th, ALU.add)
            link(pool.tensor_scalar(th, ang, PI_IN, -PI_IN, ALU.min, ALU.max))
            tt(den, lr, lr, ALU.mult)
            tt(q, LAM_IM, LAM_IM, ALU.mult)
            pool.tensor_tensor(den, den, q, ALU.add).then_inc(sem("s5_angle"), 1)
            pool.wait_ge(sem("s5_recips"), 1)
            tt(em1, tnh, tq, ALU.mult)
            tsc(em1, em1, 2.0, ALU.mult)
            tt(w, sh, sh, ALU.mult)
            tsc(w, w, -2.0, ALU.mult)
            tsc(cosv, w, 1.0, ALU.add)
            tsc(mag[:, :], em1, 1.0, ALU.add)
            tt(nr, em1, cosv, ALU.mult)
            tt(nr, nr, w, ALU.add)
            tt(ai, mag[:, :], sn, ALU.mult)
            li = LAM_IM
            tt(kr, nr, lr, ALU.mult)
            tt(q, ai, li, ALU.mult)
            tt(kr, kr, q, ALU.add)
            tt(kr, kr, den, ALU.mult)
            tt(ki, ai, lr, ALU.mult)
            tt(q, nr, li, ALU.mult)
            tt(ki, ki, q, ALU.subtract)
            tt(ki, ki, den, ALU.mult)
            pool.wait_ge(sem("s5_in"), 64)
            krb, kib = (t.unsqueeze(2).broadcast_to([P, ST, S5I]) for t in (kr, ki))
            tt(bbar[:, 0], krb, bnat[:, 0], ALU.mult)
            tt(q1[:, :, :], kib, bnat[:, 1], ALU.mult)
            tt(bbar[:, 0], bbar[:, 0], q1[:, :, :], ALU.subtract)
            tt(bbar[:, 1], krb, bnat[:, 1], ALU.mult)
            tt(q1[:, :, :], kib, bnat[:, 0], ALU.mult)
            tt(bbar[:, 1], bbar[:, 1], q1[:, :, :], ALU.add)
            tsc(e0, cosv, 1.0, ALU.mult)
            tsc(e1, sn, 1.0, ALU.mult)
            for which in (2, 0):
                cw, sw = rot[:, which], rot[:, which + 1]
                link(pool.memset(cw[:, :, 0:1], 1.0))
                link(pool.memset(sw[:, :, 0:1], 0.0))
                n = 1
                while n < 16:
                    b0, b1 = (t.unsqueeze(2).broadcast_to([P, ST, n]) for t in (e0, e1))
                    tt(q1[:, :, 0:n], cw[:, :, 0:n], b0, ALU.mult)
                    tt(q2[:, :, 0:n], sw[:, :, 0:n], b1, ALU.mult)
                    tt(cw[:, :, n:2 * n], q1[:, :, 0:n], q2[:, :, 0:n], ALU.subtract)
                    tt(q1[:, :, 0:n], cw[:, :, 0:n], b1, ALU.mult)
                    tt(q2[:, :, 0:n], sw[:, :, 0:n], b0, ALU.mult)
                    tt(sw[:, :, n:2 * n], q1[:, :, 0:n], q2[:, :, 0:n], ALU.add)
                    tt(q, e0, e1, ALU.mult)
                    tt(w, e1, e1, ALU.mult)
                    tt(e0, e0, e0, ALU.mult)
                    tt(e0, e0, w, ALU.subtract)
                    tsc(e1, q, 2.0, ALU.mult)
                    n *= 2
            pool.tensor_copy(tick[:, 0:1], ones[:, 0:1]).then_inc(sem("s5_constants"), 1)

            pool.wait_ge(sem("h_ready"), 8)
            pool.dma_start(x_kept, xT[:, :, :].rearrange("p t s -> p (t s)")).then_inc(sem("x_saved"), 16)
            pool.wait_ge(sem("h_lo"), 8)
            pool.dma_start(wdt[:, :, :], a["w_in"][0].rearrange("(k p) n -> p k n", p=P)[:, :, OFF_DT:OFF_U]
                           ).then_inc(sem("wdt_in"), 16)
            for k in range(UT):
                if k:
                    pool.wait_ge(sem("rot_rest"), k)
                hc, hn, lc, ln = (rot[:, w_, 4 * k:4 * k + 4, :] for w_ in range(4))
                big = [v_.unsqueeze(3).broadcast_to([P, 4, 16, 16]) for v_ in (hc, hn)]
                few = [v_.unsqueeze(2).broadcast_to([P, 4, 16, 16]) for v_ in (lc, ln)]
                tc4, ts4 = (t[:, :, :].rearrange("p s (j k) -> p s j k", j=16) for t in (tc, ts))
                sc4 = rscr[:, :, :].rearrange("p s (j k) -> p s j k", j=16)
                pool.tensor_tensor(sc4, big[1], few[1], ALU.mult)
                pool.tensor_tensor(tc4, big[0], few[0], ALU.mult).then_inc(sem("rot_a"), 1)
                pool.wait_ge(sem("rot_a"), k + 1)
                pool.tensor_tensor(tc4, tc4, sc4, ALU.subtract).then_inc(sem("rot_b"), 1)
                pool.wait_ge(sem("rot_b"), k + 1)
                pool.tensor_tensor(sc4, big[0], few[1], ALU.mult)
                pool.tensor_tensor(ts4, big[1], few[0], ALU.mult).then_inc(sem("rot_c"), 1)
                pool.wait_ge(sem("rot_c"), k + 1)
                pool.tensor_tensor(ts4, ts4, sc4, ALU.add).then_inc(sem("rot_ready"), 1)
            pool.wait_ge(sem("x_saved"), 16)
            pool.wait_ge(sem("prod_free"), 1 + FT // 2 + 1 + D // (COLS // 2))
            pool.dma_start(xT[:, :, :].rearrange("p t s -> p (t s)"), x_kept).then_inc(sem("x_back"), 16)

        @block.scalar
        def _(act):
            r = Run()

            def hi(lap, pos, m, mpos):
                act.wait_ge(landed(pos % RING), lap * 32 + 32)
                if not (isinstance(m, int) and m < SPLIT):
                    act.wait_ge(slab_done, m - (SPLIT - 1))
                act.activation(whi[:, mpos % SPLIT, :, :], raw[:, pos % RING, :, :], ACT.Copy).then_inc(hi_ready, 1)

            act.wait_ge(sem("rows_turned"), 1)
            act.activation(pv[:, :, :].rearrange("p a b -> p (a b)"), mps[:, 0, :], ACT.Copy).then_inc(sem("vectors"), 1)
            act.wait_ge(sem("vectors"), 1)
            act.activation(cact[:, :], C_IN, ACT.Silu).then_inc(sem("c_act"), 1)
            for t in range(4):
                act.wait_ge(sem("x_turned"), t + 1)
                act.activation(xT[:, 4 * t:4 * t + 4, :], gps[:, t % 2, :, :], ACT.Copy).then_inc(sem("x_ready"), 1)

            weights = [ph for kind, ph in steps if kind == "gemm"]
            starts, n, m = {}, 32, 0
            for ph in weights:
                starts[id(ph)] = (n, m)
                n += len(ph.stream) * ph.bodies
                m += 2 * ph.slabs * ph.bodies

            def first_two(ph, i=None, side=iter(())):
                n0, m0 = starts[id(ph)]
                per = len(ph.stream)
                for s in range(2):
                    if i is None:
                        hi(n0 // RING, s, m0 + s, s)
                    else:
                        hi(n0 // RING + (i + 1) * (per // RING), s, m0 + (i + 1) * 2 * ph.slabs + s, s)
                    next(side, None)

            def xbc_silu(group, q):
                act.wait_ge(psum_free(group % 2), q)
                t = xbc[:, 4 * group:4 * group + 4, :]
                act.activation(t, t, ACT.Silu).then_inc(sem("xbc_ready"), 1)

            def evacuate(ph, i, g, m_end, q):
                b = g
                act.wait_ge(slab_done, m_end)
                out = gps[:, b, :, :]
                if ph.evac == "pair":
                    act.wait_ge(sem("prod_free"), r.p + i * 2 + g + 1)
                    act.activation(sil[:, :, :], out[:, 0:2, :], ACT.Silu).then_inc(sem("silu_ready"), 1)
                    act.wait_ge(psum_free(b), q)
                    f = ph.start + i * 2 + g
                    k = 2
                    if ph.narrow and g == 1:
                        k = 1
                    act.activation(ffs[:, bass.ds(2 * f, k), 0, :], prod[:, 0:k, :], ACT.Copy).then_inc(sem("ff_hi"), 1)
                elif ph.evac == "conv":
                    if i or g:
                        xbc_silu(2 * i + g - 1, q - 1 + g)
                elif ph.evac in ("copy", "silu", "sig_a", "sig_b"):
                    if ph.evac == "silu" and i == 0 and g == 0:
                        xbc_silu(CT // 4 - 1, q - 1)
                    if ph.evac == "silu" and i == 1 and g == 0:
                        act.wait_ge(sem("s5_turned"), UT)
                    if ph.evac == "sig_a":
                        act.wait_ge(sem("s5_out"), UT)
                    if ph.evac == "sig_b":
                        act.wait_ge(sem("ssd_group_done"), 2 * i + g + 1)
                    dst, f = {"copy": (ub, ACT.Copy), "silu": (zb, ACT.Silu), "sig_a": (ga, ACT.Sigmoid),
                              "sig_b": (gb, ACT.Sigmoid)}[ph.evac]
                    act.activation(dst[:, bass.ds(8 * i + 4 * g, 4), :], out, f).then_inc(psum_free(b), 1)
                elif ph.evac == "glu":
                    act.wait_ge(sem("prod_free"), r.p + i * 2 + g + 1)
                    act.activation(sil[:, :, :], out[:, 2:4, :], ACT.Sigmoid).then_inc(sem("silu_ready"), 1)
                    act.wait_ge(sem("merged"), i * 2 + g + 1)
                    act.activation(hs[:, bass.ds(4 * i + 2 * g, 2), 0, :], prod[:, :, :], ACT.Copy
                                   ).then_inc(sem("ff_hi"), 1)

            def gemm(ph, following, side):
                n0, m0 = starts[id(ph)]
                per, mper = len(ph.stream), 2 * ph.slabs

                def body(i, nxt):
                    for g in range(2):
                        for pos, (what, gg, s) in enumerate(ph.stream):
                            if what == "w" and gg == g and s >= 2:
                                mp = gg * ph.slabs + s
                                hi(n0 // RING + i * (per // RING) + pos // RING, pos, m0 + i * mper + mp, mp)
                                next(side, None)
                        if g == 0:
                            for pos, (what, gg, s) in enumerate(ph.stream):
                                if what == "w" and gg == 1 and s < 2:
                                    mp = ph.slabs + s
                                    hi(n0 // RING + i * (per // RING) + pos // RING, pos, m0 + i * mper + mp, mp)
                                    next(side, None)
                        elif nxt == "loop":
                            first_two(ph, i, side)
                        elif nxt is not None:
                            first_two(nxt, side=side)
                        if g == 1:
                            if ph.side and ph.last and i == ph.bodies - 1:
                                for _ in side:
                                    pass
                        evacuate(ph, i, g, m0 + i * mper + (g + 1) * ph.slabs, r.q + i + 1)

                if ph.bodies > 1 and not ph.side:
                    with act.Fori(0, ph.bodies - 1) as i:
                        body(i, "loop")
                else:
                    for i in range(ph.bodies - 1):
                        body(i, "loop")
                body(ph.bodies - 1, following)
                r.q += ph.bodies
                if ph.evac in ("pair", "glu"):
                    r.p += 2 * ph.bodies

            def norm(k, last=False):
                act.wait_ge(sem("x_ready"), 4)
                for b in range(2):
                    if r.q:
                        act.wait_ge(psum_free(b), r.q)
                if k:
                    act.wait_ge(sem("h_lo"), 4 * k)
                    act.wait_ge(slab_done, r.m)
                if k == 1:
                    act.wait_ge(sem("s5_constants"), 1)
                for t in range(4):
                    act.activation(xw[:, 4 * t:4 * t + 4, :], xT[:, 4 * t:4 * t + 4, :], ACT.Square
                                   ).then_inc(sem("squares"), 1)
                act.wait_ge(sem("variance"), k + 1)
                act.activation(rs[:, :], var[:, :], ACT.Sqrt).then_inc(sem("deviation"), 1)
                if last:
                    return
                for t in range(4):
                    act.wait_ge(sem("h_ready"), 4 * k + t + 1)
                    act.activation(hs[:, 4 * t:4 * t + 4, 0, :], xw[:, 4 * t:4 * t + 4, :], ACT.Copy
                                   ).then_inc(sem("h_hi"), 1)

            def dt_part():
                act.wait_ge(sem("wdt_in"), 16)
                act.activation(wdth[:, :, :], wdt[:, :, :], ACT.Copy).then_inc(sem("wdt_hi"), 1)
                act.activation(hb[:, 3, :], hb[:, 0, :], ACT.Exp).then_inc(sem("a_exp"), 1)
                act.wait_ge(sem("dt_abs"), 1)
                act.activation(dta[:, :, :], dta[:, :, :], ACT.Exp, scale=-1.0).then_inc(sem("dt_exp"), 1)
                act.wait_ge(sem("dt_one_more"), 1)
                act.activation(dtv[:, :, :], dtb[:, :, :], ACT.Ln).then_inc(sem("dt_ln"), 1)
                act.wait_ge(sem("wend_arg"), 1)
                act.activation(wend[:, :, :], wend[:, :, :], ACT.Exp)
                act.activation(ecs[:, :, :], cs[:, :, :], ACT.Exp).then_inc(sem("decays"), 1)

            def ssd():
                act.wait_ge(sem("xbc_ready"), 6)
                for i in range(GROUPS):
                    act.wait_ge(sem("b_and_cb"), i + 1)
                    act.activation(btok[:, :], mps[:, 2, 0:P], ACT.Copy).then_inc(sem("b_tokens"), 1)
                    yield
                    act.wait_ge(sem("state"), i + 1)
                    act.activation(prev[:, :], mps[:, 3, :], ACT.Copy).then_inc(sem("state_kept"), 1)
                    yield
                    act.wait_ge(sem("seg_in0"), i + 1)
                    act.activation(E[0][:, :, :], E[0][:, :, :], ACT.Exp).then_inc(sem("seg_exp0"), 1)
                    yield
                    act.wait_ge(sem("y_diag0"), i + 1)
                    act.activation(ytok[:, 0, :], mps[:, 2, :], ACT.Copy).then_inc(sem("y_tok0"), 1)
                    act.wait_ge(sem("seg_in1"), i + 1)
                    act.activation(E[1][:, :, :], E[1][:, :, :], ACT.Exp).then_inc(sem("seg_exp1"), 1)
                    yield
                    yield
                    yield
                    act.wait_ge(sem("y_gated"), i + 1)
                    act.activation(E[0][:, :, :], E[1][:, :, :], ACT.Square).then_inc(sem("y_squares"), 1)
                    yield
                    act.wait_ge(sem("y_var"), i + 1)
                    act.activation(rs[:, :], var[:, :], ACT.Sqrt).then_inc(sem("y_dev"), 1)
                    yield

            def s5_mats(k):
                act.wait_ge(sem("s5_turned"), k + 1)
                act.activation(btb[:, :, :, :].rearrange("p a b c -> p (a b c)"),
                               mps[:, 0:2, :].rearrange("p a b -> p (a b)"), ACT.Copy)
                act.activation(ctb[:, :, :, :].rearrange("p a b c -> p (a b c)"),
                               mps[:, 2:4, :].rearrange("p a b -> p (a b)"), ACT.Copy).then_inc(sem("s5_mats"), 1)

            def s5():
                for k in range(UT):
                    for _ in range(4):
                        yield
                    act.wait_ge(sem("s5_y"), k + 1)
                    act.activation(ub[:, k, :], rs[:, :], ACT.Gelu_apprx_tanh).then_inc(sem("s5_gelu"), 1)
                    if k + 1 < UT:
                        s5_mats(k + 1)
                    yield

            def split():
                for b in range(2):
                    act.wait_ge(psum_free(b), r.q)
                act.wait_ge(slab_done, r.m)
                act.wait_ge(sem("ssd_group_done"), GROUPS)
                act.wait_ge(sem("s5_gelu"), UT)
                act.activation(hs[:, :, 0, :], xbc[:, 0:NT, :], ACT.Copy).then_inc(sem("y_hi"), 1)
                act.activation(ybs[:, :, 0, :], ub[:, :, :], ACT.Copy).then_inc(sem("y_hi"), 1)

            def final():
                norm(3, last=True)
                for t in range(4):
                    act.wait_ge(sem("y_turned"), 2 * t + 1)
                    act.activation(xout[:, 0, 512 * t:512 * t + 512], mps[:, 0, :], ACT.Copy).then_inc(sem("y_out"), 1)
                    act.wait_ge(sem("y_turned"), 2 * t + 2)
                    act.activation(xout[:, 1, 512 * t:512 * t + 512], mps[:, 1, :], ACT.Copy).then_inc(
                        sem("y_out") if t < 3 else sem("out_ready"), 1)

            todo = list(weights)
            sides = {"s5": s5(), "ssd": ssd()}
            for kind, ph in steps:
                if kind == "norm":
                    norm(ph)
                    if ph == 0:
                        first_two(todo[0])
                elif kind == "gemm":
                    todo.pop(0)
                    gemm(ph, todo[0] if todo else None, sides.get(ph.side, iter(())))
                    r.m += 2 * ph.slabs * ph.bodies
                elif kind == "s5_step":
                    act.wait_ge(sem("s5_logdt"), 1)
                    act.activation(sp[:, 0, :], sp[:, 1, :], ACT.Exp).then_inc(sem("s5_dt"), 1)
                elif kind == "s5_sines":
                    act.wait_ge(sem("s5_angle"), 1)
                    act.activation(sp[:, 5, :], sp[:, 4, :], ACT.Tanh, scale=0.5)
                    act.activation(sp[:, 6, :], sp[:, 3, :], ACT.Sin)
                    act.activation(sp[:, 7, :], sp[:, 3, :], ACT.Sin, scale=0.5).then_inc(sem("s5_sines"), 1)
                elif kind == "dt":
                    dt_part()
                elif kind == "s5_begin":
                    s5_mats(0)
                elif kind == "s5_end":
                    for _ in sides["s5"]:
                        pass
                elif kind == "split":
                    split()
                elif kind == "final":
                    final()

        @block.vector
        def _(dve):
            r = Run()
            chain = [0]

            def link(ins):
                ins.then_inc(sem("vector_step"), 1)
                chain[0] += 1
                dve.wait_ge(sem("vector_step"), chain[0])

            def lo(lap, pos, m, mpos):
                dve.wait_ge(hi_ready, m + 1)
                dve.tensor_tensor(wlo[:, mpos % SPLIT, :, :], raw[:, pos % RING, :, :],
                                  whi[:, mpos % SPLIT, :, :].bitcast(F32), ALU.subtract).then_inc(raw_used, 1)

            def ada_slab(lap, pos, c, s, back, first=0):
                dve.wait_ge(landed(pos % RING), lap * 32 + 32)
                for k in range(4):
                    kk = 4 * s + k
                    w = raw[:, pos % RING, k, :]
                    if kk == first:
                        ins = dve.tensor_scalar(acc[:, :], w, cact[:, kk:kk + 1], None, ALU.mult)
                    else:
                        if k:
                            dve.wait_ge(sem("ada_step"), c * 12 + 3 * s + k)
                        else:
                            dve.wait_ge(raw_used, lap * RING + pos % RING + 1 - back)
                        ins = dve.scalar_tensor_tensor(out=acc[:, :], in0=w, scalar=cact[:, kk:kk + 1], in1=acc[:, :],
                                                       op0=ALU.mult, op1=ALU.add)
                    if k < 3:
                        ins.then_inc(sem("ada_step"), 4 if first and kk == first else 1)
                    else:
                        ins.then_inc(raw_used, 2 if first and s == 1 else 1)

            def ada_end(c):
                dve.wait_ge(sem("ada_sum"), c + 1)
                dve.tensor_tensor(mods[:, bass.ds(4 * c, 4)], mps[:, 3, 0:4], B_ADA[:, bass.ds(4 * c, 4)], ALU.add
                                  ).then_inc(sem("ada_done"), 1)

            dve.wait_ge(sem("masks"), 1)
            dve.wait_ge(sem("c_act"), 1)
            dve.memset(prod[:, :, :], 0.0).then_inc(sem("prod_free"), 1)
            with dve.Fori(0, 8) as i:
                for s in range(1, 4):
                    ada_slab(i, s, i, s, 1, first=4)
                ada_end(i)
            r.c = 8

            weights = [ph for kind, ph in steps if kind == "gemm"]
            starts, n, m = {}, 32, 0
            for ph in weights:
                starts[id(ph)] = (n, m)
                n += len(ph.stream) * ph.bodies
                m += 2 * ph.slabs * ph.bodies

            def first_two(ph, i=None, side=iter(())):
                n0, m0 = starts[id(ph)]
                per = len(ph.stream)
                for s in range(2):
                    if i is None:
                        lo(n0 // RING, s, m0 + s, s)
                    else:
                        lo(n0 // RING + (i + 1) * (per // RING), s, m0 + (i + 1) * 2 * ph.slabs + s, s)
                    next(side, None)

            def evacuate(ph, i, g, m_end, q):
                b = g
                out = gps[:, b, :, :]
                if ph.evac == "pair":
                    p = r.p + i * 2 + g
                    dve.wait_ge(sem("silu_ready"), p + 1)
                    dve.tensor_tensor(prod[:, :, :], sil[:, :, :], out[:, 2:4, :], ALU.mult).then_inc(psum_free(b), 1)
                    dve.wait_ge(sem("ff_hi"), p + 1)
                    f = ph.start + i * 2 + g
                    k = 1 if ph.narrow and g == 1 else 2
                    dve.tensor_tensor(ffs[:, bass.ds(2 * f, k), 1, :], prod[:, 0:k, :],
                                      ffs[:, bass.ds(2 * f, k), 0, :].bitcast(F32), ALU.subtract
                                      ).then_inc(sem("prod_free"), 1)
                elif ph.evac == "resid":
                    dve.wait_ge(slab_done, m_end)
                    gate = hg[:, ph.gate, :]
                    for j in range(4):
                        t = 8 * i + 4 * g + j
                        xt = xT[:, bass.ds(t, 1), :].rearrange("p a s -> p (a s)")
                        ins = dve.scalar_tensor_tensor(out=xt, in0=out[:, j, :], scalar=gate[:, bass.ds(t, 1)],
                                                       in1=xt, op0=ALU.mult, op1=ALU.add)
                    ins.then_inc(psum_free(b), 1)
                elif ph.evac == "conv":
                    dve.wait_ge(slab_done, m_end)
                    for op in range(4 * KW):
                        lag, j = op // 4, op % 4
                        t = 8 * i + 4 * g + j
                        tap = CONV_W[:, bass.ds(CT * (KW - 1 - lag) + t, 1)]
                        dst = xbc[:, bass.ds(t, 1), :].rearrange("p a s -> p (a s)")
                        if lag == 0:
                            ins = dve.tensor_scalar(dst, out[:, j, :], tap, CONV_B[:, bass.ds(t, 1)],
                                                    ALU.mult, ALU.add)
                        else:
                            dve.wait_ge(sem("conv_step"), (2 * i + g) * 15 + op - 3)
                            ins = dve.scalar_tensor_tensor(out=dst[:, lag:S], in0=out[:, j, 0:S - lag], scalar=tap,
                                                           in1=dst[:, lag:S], op0=ALU.mult, op1=ALU.add)
                        ins.then_inc(sem("conv_step") if op < 15 else psum_free(b), 1)
                elif ph.evac == "mul_a":
                    dve.wait_ge(slab_done, m_end)
                    g_t = ga[:, bass.ds(8 * i + 4 * g, 4), :]
                    dve.tensor_tensor(g_t, out, g_t, ALU.mult).then_inc(psum_free(b), 1)
                elif ph.evac == "glu":
                    p = r.p + i * 2 + g
                    t = bass.ds(4 * i + 2 * g, 2)
                    dve.wait_ge(sem("silu_ready"), p + 1)
                    dve.tensor_tensor(prod[:, :, :], sil[:, :, :], out[:, 0:2, :], ALU.mult).then_inc(psum_free(b), 1)
                    dve.wait_ge(psum_free(b), q)
                    dve.tensor_tensor(prod[:, :, :], prod[:, :, :], gb[:, t, :], ALU.mult).then_inc(sem("p_b"), 1)
                    dve.wait_ge(sem("p_b"), i * 2 + g + 1)
                    dve.tensor_tensor(prod[:, :, :], prod[:, :, :], ga[:, t, :], ALU.add).then_inc(sem("merged"), 1)
                    dve.wait_ge(sem("ff_hi"), p + 1)
                    dve.tensor_tensor(hs[:, t, 1, :], prod[:, :, :], hs[:, t, 0, :].bitcast(F32), ALU.subtract
                                      ).then_inc(sem("prod_free"), 1)

            def gemm(ph, following, side):
                n0, m0 = starts[id(ph)]
                per, mper = len(ph.stream), 2 * ph.slabs
                for b in range(2):
                    if r.q:
                        dve.wait_ge(psum_free(b), r.q)
                if r.p:
                    dve.wait_ge(sem("prod_free"), r.p + 1)
                if ph.evac == "resid" and ph.gate is not None:
                    dve.wait_ge(sem("ada_done"), r.c)
                    if ph.gate == 1:
                        dve.wait_ge(sem("x_back"), 16)

                def body(i, nxt):
                    for g in range(2):
                        for pos, (what, gg, s) in enumerate(ph.stream):
                            lap = n0 // RING + i * (per // RING) + pos // RING
                            first = gg == 1 and s < 2
                            mine = (gg == 0 and s >= 2 or first) if g == 0 else (gg == 1 and s >= 2)
                            if what == "ada" and (s < 2) == (g == 0):
                                ada_slab(lap, pos, r.c + i, s, ph.back[s])
                            elif what == "w" and mine:
                                mp = gg * ph.slabs + s
                                lo(lap, pos, m0 + i * mper + mp, mp)
                                next(side, None)
                        if g == 1:
                            if nxt == "loop":
                                first_two(ph, i, side)
                            elif nxt is not None:
                                first_two(nxt, side=side)
                            if ph.side and ph.last and i == ph.bodies - 1:
                                for _ in side:
                                    pass
                        evacuate(ph, i, g, m0 + i * mper + (g + 1) * ph.slabs, r.q + i + 1)
                    if ph.ada:
                        ada_end(r.c + i)

                if ph.bodies > 1 and not ph.side:
                    with dve.Fori(0, ph.bodies - 1) as i:
                        body(i, "loop")
                else:
                    for i in range(ph.bodies - 1):
                        body(i, "loop")
                body(ph.bodies - 1, following)
                r.q += ph.bodies
                r.c += ph.ada * ph.bodies
                if ph.evac in ("pair", "glu"):
                    r.p += 2 * ph.bodies

            def gates(k):
                link(dve.tensor_scalar(hg[:, k, :], mods[:, 16 * (3 * k + 2):16 * (3 * k + 3)],
                                       1.0 if k == 1 else 0.5, None, ALU.mult))

            def norm(k, last=False):
                dve.wait_ge(sem("ada_done"), r.c)
                for b in range(2):
                    if r.q:
                        dve.wait_ge(psum_free(b), r.q)
                if not last:
                    link(dve.tensor_scalar(gm[:, k, :], mods[:, 16 * (3 * k + 1):16 * (3 * k + 2)], 1.0, None, ALU.add))
                    link(dve.tensor_tensor(gm[:, k, :], gm[:, k, :], NORMS[k], ALU.mult))
                dve.wait_ge(sem("sum_squares"), k + 1)
                dve.tensor_scalar(var[:, :], mps[:, 2, 0:S], 1.0 / D, EPS, ALU.mult, ALU.add
                                  ).then_inc(sem("variance"), 1)
                dve.wait_ge(sem("deviation"), k + 1)
                link(dve.reciprocal(rs[:, :], rs[:, :]))
                for t in range(4):
                    q = xw[:, 4 * t:4 * t + 4, :]
                    link(dve.tensor_tensor(q, xT[:, 4 * t:4 * t + 4, :],
                                           rs[:, :].unsqueeze(1).broadcast_to([P, 4, S]), ALU.mult))
                    for j in range(4):
                        f = 4 * t + j
                        if last:
                            ins = dve.tensor_scalar(xw[:, f, :], xw[:, f, :], N_FIN[:, f:f + 1], None, ALU.mult)
                        else:
                            ins = dve.tensor_scalar(xw[:, f, :], xw[:, f, :], gm[:, k, f:f + 1],
                                                    mods[:, 48 * k + f:48 * k + f + 1], ALU.mult, ALU.add)
                    ins.then_inc(sem("h_ready"), 1)
                if last:
                    return
                for t in range(4):
                    dve.wait_ge(sem("h_hi"), 4 * k + t + 1)
                    dve.tensor_tensor(hs[:, 4 * t:4 * t + 4, 1, :], xw[:, 4 * t:4 * t + 4, :],
                                      hs[:, 4 * t:4 * t + 4, 0, :].bitcast(F32), ALU.subtract
                                      ).then_inc(sem("h_lo"), 1)

            def per_head(v):
                return v.unsqueeze(2).broadcast_to([P, HPG, HD])

            def dt_part():
                dve.wait_ge(sem("wdt_hi"), 1)
                dve.tensor_tensor(wdtl[:, :, :], wdt[:, :, :], wdth[:, :, :].bitcast(F32), ALU.subtract
                                  ).then_inc(sem("wdt_lo"), 1)
                for half in range(2):
                    dve.tensor_copy(dcol[64 * half:64 * half + 64, :], hb[64 * half:64 * half + 64, 2, half:HEADS:2])
                dve.wait_ge(sem("a_exp"), 1)
                link(dve.tensor_scalar(hb[:, 3, :], hb[:, 3, :], -1.0, None, ALU.mult))
                dve.wait_ge(sem("dt_raw"), 1)
                link(dve.tensor_tensor(dtb[:, :, :], mps[:, 0, 0:64].rearrange("p (c h) -> p c h", c=2),
                                       hb[:, 1, :].unsqueeze(1).broadcast_to([P, 2, HEADS]), ALU.add))
                link(dve.tensor_scalar(dta[:, :, :], dtb[:, :, :], -1.0, None, ALU.mult))
                link(dve.tensor_tensor(dta[:, :, :], dta[:, :, :], dtb[:, :, :], ALU.max))
                link(dve.tensor_scalar(da[:, :, :], dtb[:, :, :], 0.0, None, ALU.max))
                dve.tensor_copy(tick[:, 1:2], ones[:, 0:1]).then_inc(sem("dt_abs"), 1)
                dve.wait_ge(sem("dt_exp"), 1)
                dve.tensor_scalar(dtb[:, :, :], dta[:, :, :], 1.0, None, ALU.add).then_inc(sem("dt_one_more"), 1)
                dve.wait_ge(sem("dt_one_more"), 1)
                link(dve.tensor_scalar(cs[:, :, :], dtb[:, :, :], -1.0, None, ALU.add))
                link(dve.tensor_tensor(cs[:, :, :], dta[:, :, :], cs[:, :, :], ALU.subtract))
                dve.wait_ge(sem("dt_ln"), 1)
                link(dve.reciprocal(wend[:, :, :], dtb[:, :, :]))
                link(dve.tensor_tensor(cs[:, :, :], cs[:, :, :], wend[:, :, :], ALU.mult))
                link(dve.tensor_tensor(dtv[:, :, :], dtv[:, :, :], cs[:, :, :], ALU.add))
                link(dve.tensor_tensor(dtv[:, :, :], dtv[:, :, :], da[:, :, :], ALU.add))
                dve.tensor_tensor(da[:, :, :], dtv[:, :, :], hb[:, 3, :].unsqueeze(1).broadcast_to([P, 2, HEADS]),
                                  ALU.mult).then_inc(sem("dt_a"), 1)
                dve.wait_ge(sem("dt_sums"), 1)
                two = [mps[:, w, 0:64].rearrange("p (c h) -> p c h", c=2) for w in (0, 1)]
                link(dve.tensor_copy(cs[:, :, :], two[0]))
                dve.tensor_tensor(wend[:, :, :], two[1], cs[:, :, :], ALU.subtract).then_inc(sem("wend_arg"), 1)
                dve.wait_ge(sem("decays"), 1)

            def ssd():
                for i in range(GROUPS):
                    one = i + 1
                    hsl = slice(HPG * i, HPG * i + HPG)
                    dve.wait_ge(sem("x_tokens"), one)
                    for c in range(2):
                        ins = dve.tensor_tensor(xdt[:, c, :].rearrange("p (h d) -> p h d", h=HPG),
                                                mps[:, c, :].rearrange("p (h d) -> p h d", h=HPG),
                                                per_head(dtv[:, c, hsl]), ALU.mult)
                    ins.then_inc(sem("x_dt"), 1)
                    dve.wait_ge(sem("b_tokens"), one)
                    dve.tensor_tensor(cbm[:, :, :], mps[:, 2, P:3 * P].rearrange("p (c l) -> p c l", c=2),
                                      tri[:, :].unsqueeze(1).broadcast_to([P, 2, P]), ALU.mult).then_inc(sem("cb_causal"), 1)
                    dve.wait_ge(sem("x_dt"), one)
                    dve.tensor_tensor(xde[:, :].rearrange("p (h d) -> p h d", h=HPG),
                                      xdt[:, 0, :].rearrange("p (h d) -> p h d", h=HPG),
                                      per_head(wend[:, 0, hsl]), ALU.mult).then_inc(sem("x_to_end"), 1)
                    yield

                    def seg(c):
                        dve.wait_ge(sem(f"seg{c}"), one)
                        for h in range(HPG):
                            ins = dve.tensor_scalar(E[c][:, h, :], mps[:, h // 4, P * (h % 4):P * (h % 4) + P],
                                                    cs[:, c, HPG * i + h:HPG * i + h + 1], 0.0,
                                                    ALU.subtract, ALU.min)
                        ins.then_inc(sem(f"seg_in{c}"), 1)

                    def decay(c):
                        dve.wait_ge(sem(f"seg_exp{c}"), one)
                        dve.wait_ge(sem("cb_causal"), one)
                        dve.tensor_tensor(E[c][:, :, :], E[c][:, :, :],
                                          cbm[:, c, :].unsqueeze(1).broadcast_to([P, HPG, P]), ALU.mult
                                          ).then_inc(sem(f"scores{c}"), 1)

                    seg(0)
                    yield
                    decay(0)
                    yield
                    dve.wait_ge(sem("y_off"), one)
                    dve.tensor_tensor(yof[:, :].rearrange("p (h d) -> p h d", h=HPG),
                                      mps[:, 3, :].rearrange("p (h d) -> p h d", h=HPG),
                                      per_head(ecs[:, 1, hsl]), ALU.mult).then_inc(sem("y_off_kept"), 1)
                    seg(1)
                    yield
                    decay(1)
                    yield
                    dve.wait_ge(sem("y_diag1"), one)
                    dve.wait_ge(sem("y_off_kept"), one)
                    dve.tensor_tensor(ytok[:, 1, :], mps[:, 3, :], yof[:, :], ALU.add).then_inc(sem("y_tok1"), 1)
                    yield
                    dve.wait_ge(sem("y_features"), one)
                    y = E[1][:, :, :].rearrange("p a b -> p (a b)").rearrange("p (a b) -> p a b", a=4)
                    for j in range(4):
                        t = 4 * i + j
                        ins = dve.scalar_tensor_tensor(
                            out=y[:, j, :], in0=xbc[:, t, :], scalar=dcol[:, t:t + 1],
                            in1=mps[:, j // 2, S * (j % 2):S * (j % 2) + S], op0=ALU.mult, op1=ALU.add)
                    ins.then_inc(sem("y_skip"), 1)
                    dve.wait_ge(sem("y_skip"), one)
                    dve.tensor_tensor(y, y, zb[:, 4 * i:4 * i + 4, :], ALU.mult).then_inc(sem("y_gated"), 1)
                    yield
                    dve.wait_ge(sem("y_sums"), one)
                    dve.tensor_scalar(var[:, :], mps[:, 2, 0:S], 1.0 / (HPG * HD), EPS, ALU.mult, ALU.add
                                      ).then_inc(sem("y_var"), 1)
                    dve.wait_ge(sem("y_dev"), one)
                    dve.reciprocal(rs[:, :], rs[:, :]).then_inc(sem("y_rs"), 1)
                    dve.wait_ge(sem("y_rs"), one)
                    for j in range(4):
                        t = 4 * i + j
                        ins = dve.scalar_tensor_tensor(out=xbc[:, t, :], in0=y[:, j, :], scalar=N_SSD[:, t:t + 1],
                                                       in1=rs[:, :], op0=ALU.mult, op1=ALU.mult)
                    ins.then_inc(sem("ssd_group_done"), 1)
                    yield

            def s5_blocks(k):
                if k:
                    dve.wait_ge(sem("s5_turned"), k)
                for j in range(2):
                    dve.tensor_tensor(bblk[:, j], bbar[:, j, 4 * k:4 * k + 4, :].unsqueeze(2)
                                      .broadcast_to([P, 4, 8, S5I]),
                                      maskb[:, :, :].unsqueeze(3).broadcast_to([P, 4, 8, S5I]), ALU.mult)
                    ins = dve.tensor_tensor(cblk[:, j], cnat[:, j, k:k + 1, :].broadcast_to([P, 8, S5P]),
                                            maskc[:, j, :].unsqueeze(2).broadcast_to([P, 8, S5P]), ALU.mult)
                ins.then_inc(sem("s5_blocks"), 1)

            def s5():
                C_, S_, T1, T2, WR, WI = (t[:, :, :] for t in (tc, ts, t1, t2, wr, wi))
                bu = [mps[:, 2 * j:2 * j + 2, :].rearrange("p a (b s) -> p (a b) s", b=2) for j in range(2)]
                for k in range(UT):
                    one = k + 1
                    dve.wait_ge(sem("rot_ready"), one)
                    dve.wait_ge(sem("bu_ready"), one)
                    if k:
                        dve.wait_ge(sem("s5_out"), k)
                    dve.tensor_tensor(WR, C_, bu[0], ALU.mult)
                    dve.tensor_tensor(T1, S_, bu[1], ALU.mult)
                    dve.tensor_tensor(WI, C_, bu[1], ALU.mult)
                    dve.tensor_tensor(T2, S_, bu[0], ALU.mult).then_inc(sem("unrot_products"), 1)
                    dve.wait_ge(sem("unrot_products"), one)
                    dve.tensor_tensor(WR, WR, T1, ALU.add)
                    dve.tensor_tensor(WI, WI, T2, ALU.subtract).then_inc(sem("unrotated"), 1)
                    yield
                    if k + 1 < UT:
                        s5_blocks(k + 1)
                    dve.wait_ge(sem("unrotated"), one)
                    for j in range(4):
                        m = mag[:, 4 * k + j:4 * k + j + 1].broadcast_to([P, S])
                        dve.tensor_tensor_scan(t1[:, j, :], m, wr[:, j, :], 0.0, ALU.mult, ALU.add)
                        ins = dve.tensor_tensor_scan(t2[:, j, :], m, wi[:, j, :], 0.0, ALU.mult, ALU.add)
                    ins.then_inc(sem("scanned"), 1)
                    yield
                    dve.wait_ge(sem("scanned"), one)
                    dve.tensor_tensor(WR, C_, T1, ALU.mult)
                    dve.tensor_tensor(WI, S_, T2, ALU.mult).then_inc(sem("rot_half"), 1)
                    dve.wait_ge(sem("rot_half"), one)
                    dve.tensor_tensor(WR, WR, WI, ALU.subtract).then_inc(sem("s_re"), 1)
                    yield
                    dve.tensor_tensor(S_, S_, T1, ALU.mult)
                    dve.tensor_tensor(T2, C_, T2, ALU.mult).then_inc(sem("rot_last"), 1)
                    dve.wait_ge(sem("rot_last"), one)
                    dve.wait_ge(sem("s_re"), one)
                    dve.tensor_tensor(WI, S_, T2, ALU.add).then_inc(sem("rot_rest"), 1)
                    yield
                    dve.wait_ge(sem("s5_out"), one)
                    if k:
                        dve.wait_ge(sem("s5_gelu"), k)
                    dve.scalar_tensor_tensor(out=rs[:, :], in0=ub[:, k, :], scalar=S5_D[:, k:k + 1],
                                             in1=mps[:, 0, 0:S], op0=ALU.mult, op1=ALU.add).then_inc(sem("s5_y"), 1)
                    yield

            def split():
                dve.wait_ge(sem("y_hi"), 1)
                dve.tensor_tensor(hs[:, :, 1, :], xbc[:, 0:NT, :], hs[:, :, 0, :].bitcast(F32), ALU.subtract
                                  ).then_inc(sem("y_lo"), 1)
                dve.wait_ge(sem("y_hi"), 2)
                dve.tensor_tensor(ybs[:, :, 1, :], ub[:, :, :], ybs[:, :, 0, :].bitcast(F32), ALU.subtract
                                  ).then_inc(sem("y_lo"), 1)

            todo = list(weights)
            sides = {"s5": s5(), "ssd": ssd()}
            for kind, ph in steps:
                if kind == "norm":
                    norm(ph)
                    if ph == 0:
                        first_two(todo[0])
                elif kind == "gemm":
                    todo.pop(0)
                    if ph.evac == "resid" and ph.row == 0:
                        dve.wait_ge(sem("ada_done"), r.c)
                        gates(ph.gate)
                    gemm(ph, todo[0] if todo else None, sides.get(ph.side, iter(())))
                elif kind == "s5_reciprocals":
                    dve.wait_ge(sem("s5_sines"), 1)
                    dve.wait_ge(sem("s5_angle"), 1)
                    link(dve.tensor_scalar(sp[:, 22, :], sp[:, 5, :], -1.0, 1.0, ALU.mult, ALU.add))
                    dve.reciprocal(sp[:, 22, :], sp[:, 22, :])
                    dve.reciprocal(sp[:, 13, :], sp[:, 13, :]).then_inc(sem("s5_recips"), 1)
                elif kind == "dt":
                    dt_part()
                elif kind == "s5_begin":
                    s5_blocks(0)
                    dve.wait_ge(sem("x_saved"), 16)
                elif kind == "s5_end":
                    for _ in sides["s5"]:
                        pass
                elif kind == "split":
                    split()
                elif kind == "final":
                    norm(3, last=True)

        @block.tensor
        def _(pe):
            r = Run()

            def ada_end(c, used, fresh=True):
                pe.wait_ge(raw_used, used)
                for j in range(4):
                    ins = mm(pe, mps[:, 3, j:j + 1], acc[:, P * j:P * j + P], ones[:, 0:1], fresh and j == 0, True)
                ins.then_inc(sem("ada_sum"), 1)

            pe.wait_ge(sem("masks"), 1)
            pe.wait_ge(sem("rows_in"), 14 * 16)
            for j in range(4):
                ins = pe.transpose(mps[:, 0, P * j:P * j + P], rows[:, j, :], ident[:, :])
            ins.then_inc(sem("rows_turned"), 1)
            pe.wait_ge(sem("x_in"), 16)
            for t in range(4):
                if t >= 2:
                    pe.wait_ge(sem("x_ready"), t - 1)
                for j in range(4):
                    for c in range(2):
                        f = 4 * t + j
                        ins = pe.transpose(gps[:, t % 2, j, P * c:P * c + P], xin[:, c, P * f:P * f + P], ident[:, :])
                ins.then_inc(sem("x_turned"), 1)
            pe.wait_ge(sem("x_ready"), 4)
            pe.wait_ge(sem("vectors"), 1)
            pe.wait_ge(sem("c_act"), 1)
            with pe.Fori(0, 8) as i:
                pe.wait_ge(sem("ada_done"), i)
                pe.wait_ge(landed(0), i * 32 + 32)
                for k in range(4):
                    for j in range(4):
                        ins = mm(pe, mps[:, 3, j:j + 1], raw[:, 0, k, P * j:P * j + P], cact[:, k:k + 1],
                                 k + j == 0, False)
                ins.then_inc(sem("ada_products"), 1)
                ada_end(i, i * RING + RING, fresh=False)
            r.c = 8

            def gemm(ph, n0, m0, side):
                per, mper = len(ph.stream), 2 * ph.slabs
                moving = {"h": hs, "ff": ffs, "yb": ybs}[ph.moving]
                if ph.moving == "ff":
                    pe.wait_ge(sem("prod_free"), r.p + 1)
                elif ph.name == "w_out":
                    pe.wait_ge(sem("prod_free"), r.p + 1)
                elif ph.name == "a_proj":
                    pe.wait_ge(sem("y_lo"), 1)
                elif ph.name == "b_glu":
                    pe.wait_ge(sem("y_lo"), 2)

                def body(i):
                    for g in range(2):
                        if isinstance(i, int) and r.q + i == 0:
                            pass
                        else:
                            pe.wait_ge(psum_free(g), r.q + i)
                        tiles = [0, 2] if ph.narrow and g == 1 else [0, 1, 2, 3]
                        for pos, (what, gg, s) in enumerate(ph.stream):
                            if what != "w" or gg != g:
                                continue
                            mp = g * ph.slabs + s
                            pe.wait_ge(raw_used, n0 + i * per + pos + 1)
                            k0 = sum(ph.chunks[:s])
                            if ph.moving == "h" and g == 0 and ph.name not in ("a_proj", "w_out"):
                                pe.wait_ge(sem("h_lo"), 4 * (norms[0] - 1) + s + 1)
                            for j in tiles:
                                for k in range(ph.chunks[s]):
                                    hi = whi[:, mp % SPLIT, k, P * j:P * j + P]
                                    lo = wlo[:, mp % SPLIT, k, P * j:P * j + P]
                                    xh, xl = moving[:, k0 + k, 0, :], moving[:, k0 + k, 1, :]
                                    out = gps[:, g, j, :]
                                    mm(pe, out, hi, xh, k0 + k == 0 and j % 2 == 0, False)
                                    mm(pe, out, hi, xl, False, False)
                                    ins = mm(pe, out, lo, xh, False, k0 + k == sum(ph.chunks) - 1)
                                if j < 3:
                                    next(side, None)
                            ins.then_inc(slab_done, 1)
                            next(side, None)
                    if ph.ada:
                        ada_end(r.c + i, n0 + i * per + ph.stream.index(("ada", 0, 3)) + 1)

                start = 0
                if r.q == 0:
                    body(0)
                    start = 1
                if ph.side:
                    for i in range(ph.bodies):
                        body(i)
                elif ph.bodies - start > 1:
                    with pe.Fori(start, ph.bodies) as i:
                        body(i)
                elif ph.bodies - start == 1:
                    body(start)
                r.q += ph.bodies
                r.c += ph.ada * ph.bodies
                if ph.evac in ("pair", "glu"):
                    r.p += 2 * ph.bodies

            def norm(k):
                for t in range(4):
                    pe.wait_ge(sem("squares"), 4 * k + t + 1)
                    for j in range(4):
                        f = 4 * t + j
                        ins = mm(pe, mps[:, 2, 0:S], ones[:, :], xw[:, f, :], f == 0, f == NT - 1)
                ins.then_inc(sem("sum_squares"), 1)

            def dt_part():
                pe.wait_ge(sem("ada_done"), r.c)
                pe.wait_ge(sem("wdt_lo"), 1)
                for c in range(2):
                    tok = slice(P * c, P * c + P)
                    out = mps[:, 0, HEADS * c:HEADS * c + HEADS]
                    for k in range(NT):
                        mm(pe, out, hs[:, k, 0, tok], wdth[:, k, :], k == 0 and c == 0, False)
                        mm(pe, out, hs[:, k, 1, tok], wdth[:, k, :], False, False)
                        ins = mm(pe, out, hs[:, k, 0, tok], wdtl[:, k, :], False, k == NT - 1)
                ins.then_inc(sem("dt_raw"), 1)
                pe.wait_ge(sem("dt_a"), 1)
                dav = da[:, :, :].rearrange("p c h -> p (c h)")
                mm(pe, mps[:, 0, 0:64], tri[:, :], dav, True, True)
                mm(pe, mps[:, 1, 0:64], ones[:, :], dav, True, True).then_inc(sem("dt_sums"), 1)

            def ssd():
                c_start = r.c
                for i in range(GROUPS):
                    one = i + 1

                    def seg(c):
                        for h in range(HPG):
                            ins = mm(pe, mps[:, h // 4, P * (h % 4):P * (h % 4) + P],
                                     da[:, c, HPG * i + h:HPG * i + h + 1].broadcast_to([P, P]), tri[:, :],
                                     h % 4 == 0, h % 4 == 3)
                        ins.then_inc(sem(f"seg{c}"), 1)

                    def diag(c):
                        pe.wait_ge(sem(f"scores{c}"), one)
                        for h in range(HPG):
                            ins = mm(pe, mps[:, 2 + c, HD * h:HD * h + HD], E[c][:, h, :], xdt[:, c, HD * h:HD * h + HD],
                                     h == 0, h == HPG - 1)
                        ins.then_inc(sem(f"y_diag{c}"), 1)

                    def quarters_of_gates(count):
                        for _ in range(count):
                            yield

                    b_t, c_t = xbc[:, 4 * GROUPS + i, :], xbc[:, 5 * GROUPS + i, :]
                    yield from quarters_of_gates(2 if i else 4)
                    if i == 0:
                        pe.wait_ge(sem("xbc_ready"), 6)
                        pe.wait_ge(sem("s5_y"), UT)
                        pe.wait_ge(sem("ada_done"), r.c)
                    else:
                        pe.wait_ge(sem("y_gated"), i)
                        pe.wait_ge(sem("y_var"), i)
                    for c in range(2):
                        for j in range(4):
                            ins = pe.transpose(mps[:, c, P * j:P * j + P], xbc[:, 4 * i + j, P * c:P * c + P], ident[:, :])
                    ins.then_inc(sem("x_tokens"), 1)
                    pe.transpose(mps[:, 2, 0:P], b_t[:, 0:P], ident[:, :])
                    for c in range(2):
                        tok = slice(P * c, P * c + P)
                        ins = mm(pe, mps[:, 2, P * (c + 1):P * (c + 2)], b_t[:, tok], c_t[:, tok], c == 0, c == 1)
                    ins.then_inc(sem("b_and_cb"), 1)
                    yield from quarters_of_gates(5)
                    pe.wait_ge(sem("x_dt"), one)
                    seg(0)
                    pe.wait_ge(sem("x_to_end"), one)
                    pe.wait_ge(sem("b_tokens"), one)
                    if i:
                        pe.wait_ge(sem("ada_done"), c_start + i)
                    mm(pe, mps[:, 3, :], btok[:, :], xde[:, :], True, True).then_inc(sem("state"), 1)
                    yield from quarters_of_gates(4)
                    pe.wait_ge(sem("state_kept"), one)
                    mm(pe, mps[:, 3, :], c_t[:, P:2 * P], prev[:, :], True, True).then_inc(sem("y_off"), 1)
                    pe.wait_ge(sem("seg_in0"), one)
                    seg(1)
                    yield from quarters_of_gates(4)
                    diag(0)
                    yield from quarters_of_gates(8)
                    pe.wait_ge(sem("y_off_kept"), one)
                    diag(1)
                    yield from quarters_of_gates(3)
                    pe.wait_ge(sem("y_tok0"), one)
                    pe.wait_ge(sem("y_tok1"), one)
                    for j in range(4):
                        for c in range(2):
                            at_ = S * (j % 2) + P * c
                            ins = pe.transpose(mps[:, j // 2, at_:at_ + P], ytok[:, c, P * j:P * j + P], ident[:, :])
                    ins.then_inc(sem("y_features"), 1)
                    yield from quarters_of_gates(6)
                    pe.wait_ge(sem("y_squares"), one)
                    sq = E[0][:, :, :].rearrange("p a b -> p (a b)")
                    for j in range(4):
                        ins = mm(pe, mps[:, 2, 0:S], ones[:, :], sq[:, S * j:S * j + S], j == 0, j == 3)
                    ins.then_inc(sem("y_sums"), 1)

            def s5_turn(k):
                pe.wait_ge(sem("s5_blocks"), k + 1)
                if k:
                    pe.wait_ge(sem("unrot_products"), k)
                bf = bblk[:, :, :, :, :].rearrange("p r j g i -> p (r j) (g i)")
                cf = cblk[:, :, :, :].rearrange("p r g s -> p (r g s)")
                for t in range(8):
                    pe.transpose(mps[:, t // 4, P * (t % 4):P * (t % 4) + P], bf[:, t, :], ident[:, :])
                    ins = pe.transpose(mps[:, 2 + t // 4, P * (t % 4):P * (t % 4) + P], cf[:, P * t:P * t + P],
                                       ident[:, :])
                ins.then_inc(sem("s5_turned"), 1)

            def s5_bu(k):
                pe.wait_ge(sem("s5_mats"), k + 1)
                if k:
                    pe.wait_ge(sem("s5_y"), k)
                for rim in range(2):
                    for j in range(4):
                        ins = mm(pe, mps[:, 2 * rim + j // 2, S * (j % 2):S * (j % 2) + S], btb[:, rim, j, :],
                                 ub[:, k, :], j % 2 == 0, j % 2 == 1)
                ins.then_inc(sem("bu_ready"), 1)

            def s5():
                for k in range(UT):
                    for _ in range(21 if k == 0 else 15):
                        yield
                    for rim, states in enumerate((wr, wi)):
                        pe.wait_ge(sem("s_re" if rim == 0 else "rot_rest"), k + 1)
                        for j in range(4):
                            ins = mm(pe, mps[:, 0, 0:S], ctb[:, rim, j, :], states[:, j, :], rim + j == 0,
                                     rim == 1 and j == 3)
                    ins.then_inc(sem("s5_out"), 1)
                    if k + 1 < UT:
                        yield
                        yield
                        pe.wait_ge(sem("s5_y"), k + 1)
                        s5_turn(k + 1)
                        for _ in range(3):
                            yield
                        s5_bu(k + 1)

            def final():
                norm(3)
                for t in range(4):
                    pe.wait_ge(sem("h_ready"), 12 + t + 1)
                    for c in range(2):
                        if t or c:
                            if t:
                                pe.wait_ge(sem("y_out"), 2 * (t - 1) + c + 1)
                        for j in range(4):
                            ins = pe.transpose(mps[:, c, P * j:P * j + P], xw[:, 4 * t + j, P * c:P * c + P], ident[:, :])
                        ins.then_inc(sem("y_turned"), 1)

            n, m = 32, 0
            sides = {"s5": s5(), "ssd": ssd()}
            norms = [0]
            for kind, ph in steps:
                if kind == "norm":
                    norm(ph)
                    norms[0] += 1
                elif kind == "gemm":
                    gemm(ph, n, m, sides.get(ph.side, iter(())))
                    n += len(ph.stream) * ph.bodies
                    m += 2 * ph.slabs * ph.bodies
                elif kind == "dt":
                    dt_part()
                elif kind == "s5_begin":
                    s5_turn(0)
                    s5_bu(0)
                elif kind in ("s5_end", "split"):
                    for _ in sides["s5" if kind == "s5_end" else "ssd"]:
                        pass
                elif kind == "final":
                    final()


_INS = ["x", "c", "w_ada", "b_ada", "norm_ffn1", "w_ffn1_in", "w_ffn1_out", "norm_mix", "w_in", "conv_w", "conv_b",
        "dt_bias", "a_log", "d_ssd", "ssd_norm_w", "w_a_proj", "s5_lambda_re", "s5_lambda_im", "s5_b_re", "s5_b_im",
        "s5_c_re", "s5_c_im", "s5_d", "s5_log_dt", "w_b_glu", "w_out", "norm_ffn2", "w_ffn2_in", "w_ffn2_out",
        "norm_final"]


def kernel(**inputs):
    import numpy as np
    import concourse.bacc as bacc
    from concourse.bass_utils import run_bass_kernel_spmd

    nc = bacc.Bacc("TRN2", target_bir_lowering=False, num_devices=1)
    arrays, aps = {}, {}
    for name in _INS:
        v = np.ascontiguousarray(inputs[name])
        arrays[f"in_{name}_dram"] = v
        aps[name] = nc.dram_tensor(f"in_{name}_dram", v.shape, mybir.dt.from_np(v.dtype), kind="ExternalInput").ap()
    aps["out"] = nc.dram_tensor("out_dram", (1, S, D), F32, kind="ExternalOutput").ap()
    build(nc, aps)
    r = run_bass_kernel_spmd(nc, [arrays], core_ids=[0])
    return r.results[0]["out_dram"]
```
